# Optimizing a Trainium2 kernel written in Bass

```python
import jax, jax.numpy as jnp
from jax import lax
import numpy as np

D_MODEL = 2048
BATCH = 1
SEQ = 512
DEPTH = 2

N_EVEN = (DEPTH + 1) // 2
N_ODD = DEPTH // 2
W_A = D_MODEL // 2
W_B = D_MODEL // 2
HEAD_DIM = 64
CONV_A = 3
CONV_B = 31
W_C = D_MODEL
POOL_WINDOWS = (2, 4, 8, 16)
N_POOL_GROUPS = len(POOL_WINDOWS)
G_C = W_C // N_POOL_GROUPS
EVEN_IN = 4 * W_A + 3 * W_B
ODD_IN = 2 * W_C
EPS = 1e-6

kernel_name = "hybrid_shortconv_conformer_pool_sandwich"

def _rmsnorm(x, g):
    xf = x.astype(jnp.float32)
    r = lax.rsqrt(jnp.mean(xf * xf, axis=-1, keepdims=True) + EPS)
    return (xf * r).astype(x.dtype) * g

def _layernorm(x, g, b):
    xf = x.astype(jnp.float32)
    mu = jnp.mean(xf, axis=-1, keepdims=True)
    var = jnp.mean(jnp.square(xf - mu), axis=-1, keepdims=True)
    return ((xf - mu) * lax.rsqrt(var + EPS)).astype(x.dtype) * g + b

def _causal_dwconv(x, w):
    k, c = w.shape
    return lax.conv_general_dilated(
        x, w[:, None, :].astype(x.dtype), window_strides=(1,),
        padding=[(k - 1, 0)], dimension_numbers=("NWC", "WIO", "NWC"),
        feature_group_count=c)

def _causal_pool_means(v):
    s = v.shape[1]
    cs = jnp.cumsum(v.astype(jnp.float32), axis=1)
    pos = jnp.arange(1, s + 1, dtype=jnp.int32)
    outs = []
    for win, c in zip(POOL_WINDOWS, jnp.split(cs, N_POOL_GROUPS, axis=-1)):
        shifted = jnp.pad(c, ((0, 0), (win, 0), (0, 0)))[:, :s]
        cnt = jnp.minimum(pos, win).astype(jnp.float32)[None, :, None]
        outs.append((c - shifted) / cnt)
    return jnp.concatenate(outs, axis=-1).astype(v.dtype)

def _even_mixer(h, w_in, a_conv, b_conv, b_conv_bias, b_ln_g, b_ln_b, w_out):
    p = h @ w_in
    a_x, a_b, a_c, a_z, b_val, b_gate, b_z = jnp.split(p, 7, axis=-1)
    ya = a_b * _causal_dwconv(a_c * a_x, a_conv)
    yb = b_val * jax.nn.sigmoid(b_gate)
    yb = _causal_dwconv(yb, b_conv) + b_conv_bias
    yb = jax.nn.silu(_layernorm(yb, b_ln_g, b_ln_b))
    u = jnp.concatenate([ya * jax.nn.silu(a_z), yb * jax.nn.silu(b_z)], axis=-1)
    return u @ w_out

def _odd_mixer(h, w_in, c_w, c_b, c_scale, w_out):
    p = h @ w_in
    v, z = jnp.split(p, 2, axis=-1)
    pooled = _causal_pool_means(v) - v
    bsz, s, _ = v.shape
    g = pooled.reshape(bsz, s, N_POOL_GROUPS, G_C)
    g = jnp.einsum("bsgc,gcd->bsgd", g, c_w) + c_b
    y = g.reshape(bsz, s, W_C) * c_scale
    return (y * jax.nn.silu(z)) @ w_out

def setup_inputs(seed: int = 0) -> dict:
    key = jax.random.key(seed)
    ks = jax.random.split(key, 24)
    f32 = jnp.float32

    def nrm(k, shape, scale):
        return jax.random.normal(k, shape, f32) * scale

    def gain(k, shape):
        return 1.0 + 0.05 * jax.random.normal(k, shape, f32)

    return {
        "x": jax.random.normal(ks[0], (BATCH, SEQ, D_MODEL), f32),
        "e_norm_pre": gain(ks[1], (N_EVEN, D_MODEL)),
        "e_norm_post": gain(ks[2], (N_EVEN, D_MODEL)),
        "e_w_in": nrm(ks[3], (N_EVEN, D_MODEL, EVEN_IN), D_MODEL ** -0.5),
        "e_a_conv": nrm(ks[4], (N_EVEN, CONV_A, W_A), CONV_A ** -0.5),
        "e_b_conv": nrm(ks[5], (N_EVEN, CONV_B, W_B), CONV_B ** -0.5),
        "e_b_conv_bias": nrm(ks[6], (N_EVEN, W_B), 0.02),
        "e_b_ln_g": gain(ks[7], (N_EVEN, W_B)),
        "e_b_ln_b": nrm(ks[8], (N_EVEN, W_B), 0.02),
        "e_w_out": nrm(ks[9], (N_EVEN, W_A + W_B, D_MODEL), (W_A + W_B) ** -0.5),
        "o_norm_pre": gain(ks[10], (N_ODD, D_MODEL)),
        "o_norm_post": gain(ks[11], (N_ODD, D_MODEL)),
        "o_w_in": nrm(ks[12], (N_ODD, D_MODEL, ODD_IN), D_MODEL ** -0.5),
        "o_c_w": nrm(ks[13], (N_ODD, N_POOL_GROUPS, G_C, G_C), G_C ** -0.5),
        "o_c_b": nrm(ks[14], (N_ODD, N_POOL_GROUPS, G_C), 0.02),
        "o_c_scale": gain(ks[15], (N_ODD, W_C)),
        "o_w_out": nrm(ks[16], (N_ODD, W_C, D_MODEL), W_C ** -0.5),
    }

def reference(x, e_norm_pre, e_norm_post, e_w_in, e_a_conv, e_b_conv, e_b_conv_bias,
              e_b_ln_g, e_b_ln_b, e_w_out, o_norm_pre, o_norm_post, o_w_in, o_c_w,
              o_c_b, o_c_scale, o_w_out):
    for layer in range(DEPTH):
        i = layer // 2
        if layer % 2 == 0:
            h = _rmsnorm(x, e_norm_pre[i])
            y = _even_mixer(h, e_w_in[i], e_a_conv[i], e_b_conv[i], e_b_conv_bias[i],
                            e_b_ln_g[i], e_b_ln_b[i], e_w_out[i])
            x = x + _rmsnorm(y, e_norm_post[i])
        else:
            h = _rmsnorm(x, o_norm_pre[i])
            y = _odd_mixer(h, o_w_in[i], o_c_w[i], o_c_b[i], o_c_scale[i], o_w_out[i])
            x = x + _rmsnorm(y, o_norm_post[i])
    return x


_drawn_inputs = setup_inputs


def setup_inputs(seed=0):
    import zlib

    import numpy as np

    out = dict(_drawn_inputs(seed))
    spreads = {}
    factors = {'e_b_conv_bias': 3.101, 'e_b_ln_b': 6.75}
    for name, (base, spread) in spreads.items():
        noise = np.random.default_rng([zlib.crc32(name.encode()), seed]).standard_normal(out[name].shape)
        drawn = base * np.exp(spread * noise) if base else spread * noise
        out[name] = __import__('jax').numpy.asarray(drawn.astype(out[name].dtype))
    for name, factor in factors.items():
        out[name] = (out[name] * factor).astype(out[name].dtype)
    return out
```

```python
from contextlib import ExitStack

import numpy as np

import concourse.bass as bass
from concourse import mybir

F32 = mybir.dt.float32
F32R = mybir.dt.float32r
BF16 = mybir.dt.bfloat16
ALU = mybir.AluOpType
ACT = mybir.ActivationFunctionType
AX = mybir.AxisListType

P = 128
D = 2048
T = 512
TT = T // P
KT = D // P
W_A = D // 2
CB = W_A // P
CONV_A, CONV_B = 3, 31
WINDOWS = (2, 4, 8, 16)
NG = len(WINDOWS)
G_C = D // NG
EPS = 1e-6

SLAB = 2048
SLOTS = 4
RAW = 2
LOOKAHEAD = SLOTS - 1
NBLK = D // T
PAD = 32

E1A = CB
E1B = CB // 2
E1C = CB // 4
E1 = E1A + E1B + E1C
E2 = NBLK
O1V = O1Z = KT // 4
O1C = 1
O2 = NBLK
AT_E2 = E1
AT_O1 = AT_E2 + E2
AT_O1C = AT_O1 + O1V + O1Z
AT_O2 = AT_O1C + O1C
STEPS = AT_O2 + O2
LAST = SLOTS * STEPS

A_X, A_B, A_C, A_Z, B_VAL, B_GATE, B_Z = (n * W_A for n in range(7))

PRE0 = 0
MID = TT
POST1 = 3 * TT
SETS = 4 * TT
TILES_SQUARED = [PRE0 + t for t in range(TT)] + [MID + 2 * t + 1 for t in range(TT)]

VECTORS = (("conv_b", CB * CONV_B), ("conv_a", CB * CONV_A), ("bias_b", CB), ("ln_g", CB),
           ("ln_b", CB), ("c_b", KT), ("c_scale", KT))
AT_VEC = {name: sum(n for _, n in VECTORS[:i]) for i, (name, _) in enumerate(VECTORS)}
NVEC = sum(n for _, n in VECTORS)


def build(nc, x, vec, e_pre, e_post, e_in, e_out, o_pre, o_post, o_in, o_cw, o_out, out):
    ctx = ExitStack()
    with ctx:
        def sb(name, shape, dt=F32):
            return ctx.enter_context(nc.sbuf_tensor(name, shape, dt))

        def sem(name):
            return ctx.enter_context(nc.semaphore(name))

        h_hi = sb("h_hi", [P, KT, T], F32R)
        h_lo = sb("h_lo", [P, KT, T], F32R)
        rows = sb("rows", [P, KT, T])
        tok = rows[:, :, :].rearrange("p (t a) c -> p t (a c)", t=TT)
        raw = sb("raw", [P, RAW, SLAB])
        w_hi = sb("w_hi", [P, SLOTS, SLAB], F32R)
        w_lo = sb("w_lo", [P, SLOTS, SLAB], F32R)
        scratch = sb("scratch", [P, KT * T])
        shifted = sb("shifted", [P, 3, PAD + T])
        vecs = sb("vecs", [P, NVEC])
        ident = sb("ident", [P, P])
        ones = sb("ones", [P, P])
        inv_count = sb("inv_count", [P, WINDOWS[-1]])
        minus_half = sb("minus_half", [P, 1])
        junk = sb("junk", [P, 2, T], BF16)
        sumsq = sb("sumsq", [P, SETS, NBLK])
        total = sb("total", [P, SETS])
        meansq = sb("meansq", [P, SETS])
        rstd = sb("rstd", [P, SETS])

        gain_pre = scratch[:, 0:D]
        sig, a_c, csum, mean, vsum, ln_rstd, var, sq, sz0, sz1 = (
            scratch[:, D + n * T:D + (n + 1) * T] for n in range(10))
        sz = (sz0, sz1)
        gain_post, gain_next, resid0, resid1 = (scratch[:, n * D:(n + 1) * D] for n in range(4))
        resid = (resid0, resid1)
        silu_z = scratch[:, :].rearrange("p (j t) -> p j t", j=KT)

        glu, prod = shifted[:, 0, :], shifted[:, 1, :]
        v_row, sum_a, sum_b = (shifted[:, n, :] for n in range(3))
        junk_y = [shifted[:, t // 2, PAD:].bitcast(BF16)[:, t % 2 * T:(t % 2 + 1) * T]
                  for t in range(TT)]

        bank = [ctx.enter_context(nc.psum_tensor(f"bank{b}", [P, T], F32)) for b in range(8)]

        x_mid = nc.dram_tensor("x_mid", [T, D], F32, kind="Internal").ap()

        x_loaded = [sem(f"x_loaded{t}") for t in range(TT)]
        vec_loaded = sem("vec_loaded")
        gain_pre_loaded = sem("gain_pre_loaded")
        gain_end_loaded = sem("gain_end_loaded")
        resid_loaded = [sem(f"resid_loaded{s}") for s in range(2)]
        mid_stored = sem("mid_stored")
        out_stored = sem("out_stored")
        consts_set = sem("consts_set")
        pool_done = sem("pool_done")
        raw_loaded = [sem(f"raw_loaded{s}") for s in range(RAW)]
        hi_ready = sem("hi_ready")
        lo_ready = sem("lo_ready")
        slab_done = sem("slab_done")
        acc_ready = sem("acc_ready")
        bank_free = [sem(f"bank_free{b}") for b in range(8)]
        transposed = sem("transposed")
        stat_ready = sem("stat_ready")
        squared = sem("squared")
        mean_squared = sem("mean_squared")
        rstd_ready = sem("rstd_ready")
        normed = sem("normed")
        h_hi_ready = sem("h_hi_ready")
        dve_done = sem("dve_done")
        seeded_b = sem("seeded_b")
        seeded_a = sem("seeded_a")
        conv_done = sem("conv_done")
        csum_ready = sem("csum_ready")
        vsum_ready = sem("vsum_ready")
        ln_rstd_ready = sem("ln_rstd_ready")
        ln_scaled = sem("ln_scaled")
        ln_silu = sem("ln_silu")
        gated = sem("gated")
        u_hi_ready = sem("u_hi_ready")
        u_lo_ready = sem("u_lo_ready")
        y_squared = sem("y_squared")
        x_mid_ready = sem("x_mid_ready")
        z_scaled = sem("z_scaled")
        v_used = sem("v_used")
        pool_hi_ready = sem("pool_hi_ready")
        pool_lo_ready = sem("pool_lo_ready")
        out_ready = sem("out_ready")

        def f32(ap):
            return ap.bitcast(F32)

        def col(name, n, step=1):
            return vecs[:, bass.ds(n * step + AT_VEC[name], 1)]

        def tap(name, c, taps, j):
            return vecs[:, bass.ds(c * taps + (AT_VEC[name] + j), 1)]

        def tile(n):
            if isinstance(n, int):
                return rows[:, n, :]
            return rows[:, bass.ds(n, 1), :].rearrange("p a t -> p (a t)")

        def done(n):
            return n + SLOTS

        def uses4(b, part, n=0):
            stat = 1 if b < 6 else 0
            return {"start": 0, "stat": TT, "mid": TT + stat, "map": 2 * TT + stat}[part] + n

        def part4(ap, j):
            return ap[:, j * T:(j + 1) * T]

        block = ctx.enter_context(nc.Block())

        @block.sync
        def _(sp):
            sp.dma_start(gain_pre, e_pre.to_broadcast([P, D])).then_inc(gain_pre_loaded, 16)

            def load(slot, src, n=None):
                if n is not None:
                    sp.wait_ge(lo_ready, n - (RAW - 1))
                dst = raw[:, slot % RAW, :].rearrange("p (k c) -> p k c", c=src.shape[-1])
                sp.dma_start(dst, src).then_inc(raw_loaded[slot % RAW], 16)

            def columns(w, first):
                return w.rearrange("(k p) n -> p k n", p=P)[:, :, bass.ds(first, P)]

            def block_part(w, nb, q):
                v = w.rearrange("(k p) n -> p k n", p=P)
                return v[:, q * KT // 4:(q + 1) * KT // 4, bass.ds(nb * T, T)]

            E1A_ORDER = (B_GATE, B_VAL, A_C, A_X)
            for q, kind in enumerate(E1A_ORDER):
                load(q, columns(e_in, kind), q if q >= RAW else None)
                if q == RAW - 1:
                    sp.dma_start(vecs[:, :], vec).then_inc(vec_loaded, 16)
            with sp.Fori(0, E1A - 1) as i:
                for q, kind in enumerate(E1A_ORDER):
                    load(q, columns(e_in, i * P + (P + kind)), i * SLOTS + (SLOTS + q))
            with sp.Fori(0, E1B) as i:
                for q, kind in enumerate((A_B, A_Z, A_B + P, A_Z + P)):
                    load(q, columns(e_in, i * (2 * P) + kind), i * SLOTS + (E1A * SLOTS + q))
            with sp.Fori(0, E1C) as i:
                for q in range(SLOTS):
                    load(q, columns(e_in, i * (4 * P) + (B_Z + q * P)),
                         i * SLOTS + ((E1A + E1B) * SLOTS + q))

            def token_major_loads(w, step, gains, rows_in, u_tiles):
                for q in range(SLOTS):
                    load(q, block_part(w, 0, q), step * SLOTS + q)
                sp.wait_ge(u_lo_ready, u_tiles)
                for dst, src in gains:
                    sp.dma_start(dst, src.to_broadcast([P, D])).then_inc(gain_end_loaded, 16)
                for t in range(2):
                    sp.dma_start(resid[t], rows_in[t * P:(t + 1) * P, :])\
                        .then_inc(resid_loaded[t], 16)
                with sp.Fori(1, NBLK) as nb:
                    for q in range(SLOTS):
                        load(q, block_part(w, nb, q), nb * SLOTS + (step * SLOTS + q))

            token_major_loads(e_out, AT_E2, ((gain_post, e_post), (gain_next, o_pre)), x, KT)
            with sp.Fori(0, O1V + O1Z) as g:
                for q in range(SLOTS):
                    load(q, columns(o_in, g * (4 * P) + q * P), g * SLOTS + (AT_O1 * SLOTS + q))
            for g in range(NG):
                load(g, o_cw[g].rearrange("(k p) n -> p k n", p=P), AT_O1C * SLOTS + g)
            token_major_loads(o_out, AT_O2, ((gain_post, o_post),), x_mid, 2 * KT)
            for t in range(TT):
                sp.wait_ge(out_ready, 4 * t + 4)
                sp.dma_start(out[t * P:(t + 1) * P, :], tok[:, t, :]).then_inc(out_stored, 16)
            sp.wait_ge(out_stored, 16 * TT)

        @block.gpsimd
        def _(pool):
            for b in range(8):
                pool.sem_inc(bank_free[b], 1)
            pool.sem_inc(gated, 2)
            pool.sem_inc(v_used, 1)
            nc.gpsimd.memset(ident[:, :], 0.0).then_inc(pool_done, 1)
            pool.wait_ge(pool_done, 1)
            nc.gpsimd.affine_select(out=ident[:, :], in_=ident[:, :], compare_op=ALU.not_equal,
                                    fill=1.0, base=0, pattern=[[-1, P]],
                                    channel_multiplier=1).then_inc(consts_set, 1)
            nc.gpsimd.memset(minus_half[:, :], -0.5).then_inc(consts_set, 1)
            nc.gpsimd.memset(ones[:, :], 1.0).then_inc(consts_set, 1)
            nc.gpsimd.memset(shifted[:, :, 0:PAD], 0.0).then_inc(consts_set, 1)
            nc.gpsimd.memset(csum, 0.0).then_inc(consts_set, 1)
            nc.gpsimd.memset(vsum, 0.0).then_inc(consts_set, 1)
            for n in range(WINDOWS[-1]):
                nc.gpsimd.memset(inv_count[:, n:n + 1], 1.0 / (n + 1)).then_inc(consts_set, 1)
            pool.wait_ge(consts_set, 6)

            def powers(first, count):
                for n in range(first, first + count):
                    pool.wait_ge(mean_squared, n + 1)
                    nc.gpsimd.tensor_tensor(rstd[:, n:n + 1], meansq[:, n:n + 1],
                                            minus_half[:, :], ALU.pow).then_inc(rstd_ready, 1)

            powers(PRE0, TT)

            for c in range(CB):
                pool.wait_ge(conv_done, c + 1)
                nc.gpsimd.tensor_tensor(csum, csum, tile(c + CB), ALU.add)\
                    .then_inc(csum_ready, 1)
                pool.wait_ge(csum_ready, c + 1)

            pool.wait_ge(bank_free[4], uses4(4, "stat") + 2)
            for c in range(CB):
                nc.gpsimd.tensor_tensor(tile(c + CB), tile(c + CB), mean, ALU.subtract)\
                    .then_inc(pool_done, 1)
                pool.wait_ge(pool_done, c * 2 + 2)
                nc.gpsimd.tensor_tensor(sq, tile(c + CB), tile(c + CB), ALU.mult)\
                    .then_inc(pool_done, 1)
                pool.wait_ge(pool_done, c * 2 + 3)
                nc.gpsimd.tensor_tensor(vsum, vsum, sq, ALU.add).then_inc(vsum_ready, 1)
                pool.wait_ge(vsum_ready, c + 1)

            pool.wait_ge(bank_free[5], uses4(5, "stat") + 2)
            nc.gpsimd.tensor_tensor(ln_rstd, var, minus_half[:, 0:1].to_broadcast([P, T]),
                                    ALU.pow).then_inc(ln_rstd_ready, 1)

            powers(MID, 2 * TT)

            for k in range(KT):
                pool.wait_ge(pool_hi_ready, k + 1)
                nc.gpsimd.tensor_tensor(h_lo[:, k, :], rows[:, k, :], f32(h_hi[:, k, :]),
                                        ALU.subtract).then_inc(pool_lo_ready, 1)

            powers(POST1, TT)

        @block.tensor
        def _(pe):
            pe.sem_inc(slab_done, SLOTS)
            pe.wait_ge(consts_set, 3)

            def product(dst, w, m, first, last):
                nc.tensor.matmul(dst, w[0], m[0], start=first, stop=False)
                nc.tensor.matmul(dst, w[0], m[1], start=False, stop=False)
                return nc.tensor.matmul(dst, w[1], m[0], start=False, stop=last)

            def weights(slot, k, width):
                return (w_hi[:, slot, k * width:(k + 1) * width],
                        w_lo[:, slot, k * width:(k + 1) * width])

            def operand(k, first=0, width=T):
                return h_hi[:, k, first:first + width], h_lo[:, k, first:first + width]

            def feature_major(step):
                for q in range(SLOTS):
                    pe.wait_ge(lo_ready, step * SLOTS + (q + 1))
                    pe.wait_ge(bank_free[q], step + 1)
                    for k in range(KT):
                        last = product(bank[q][:, :], weights(q, k, P), operand(k),
                                       k == 0, k == KT - 1)
                    last.then_inc(slab_done, 1)

            def transposes(part, t, row):
                n = t + (TT if part == "mid" else 0)
                for j in range(4):
                    pe.wait_ge(normed, 4 * n + j + 1)
                    pe.wait_ge(bank_free[4 + j], uses4(4 + j, part, t) + 1)
                    for i in range(4):
                        k = 4 * j + i
                        last = nc.tensor.transpose(bank[4 + j][:, i * P:(i + 1) * P],
                                                   row[:, k * P:(k + 1) * P], ident[:, :])
                    last.then_inc(transposed, 1)

            def h_split(part):
                for b in range(4, 8):
                    pe.wait_ge(bank_free[b], uses4(b, part, TT) + 1)

            for t in range(TT):
                transposes("start", t, tok[:, t, :])
            h_split("start")
            with pe.Fori(0, E1A + 1) as i:
                feature_major(i)
            pe.wait_ge(csum_ready, CB)
            pe.wait_ge(bank_free[4], uses4(4, "stat") + 1)
            nc.tensor.matmul(bank[4][:, :], ones[:, :], csum, start=True, stop=True)\
                .then_inc(stat_ready, 1)
            with pe.Fori(E1A + 1, E1A + 3) as i:
                feature_major(i)
            pe.wait_ge(vsum_ready, CB)
            pe.wait_ge(bank_free[5], uses4(5, "stat") + 1)
            nc.tensor.matmul(bank[5][:, :], ones[:, :], vsum, start=True, stop=True)\
                .then_inc(stat_ready, 1)
            with pe.Fori(E1A + 3, E1) as i:
                feature_major(i)

            def token_major(step, extra, u_first):
                for q in range(SLOTS):
                    pe.wait_ge(lo_ready, step * SLOTS + (q + 1))
                    for kk in range(4):
                        k = 4 * q + kk
                        pe.wait_ge(u_lo_ready, u_first + k + 1)
                        for t in range(TT):
                            if k == 0:
                                pe.wait_ge(bank_free[t], step + (1 + extra))
                            last = product(bank[t][:, :], operand(k, t * P, P),
                                           weights(q, kk, T), k == 0, k == KT - 1)
                            if k == KT - 1 and t < TT - 1:
                                last.then_inc(acc_ready, 1)
                    last.then_inc(slab_done, 1)

            def token_major_last(step, extra, between):
                for t in range(TT):
                    pe.wait_ge(bank_free[t], step + 1 + extra)
                    for q in range(SLOTS):
                        if t == 0:
                            pe.wait_ge(lo_ready, step * SLOTS + q + 1)
                        for kk in range(4):
                            k = 4 * q + kk
                            last = product(bank[t][:, :], operand(k, t * P, P),
                                           weights(q, kk, T), k == 0, k == KT - 1)
                        if t == TT - 1:
                            last.then_inc(slab_done, 1)
                    if t < TT - 1:
                        last.then_inc(acc_ready, 1)
                    between(t)

            def mid_transposes(t):
                if t > 0:
                    transposes("mid", t - 1, resid[(t - 1) % 2])

            with pe.Fori(0, NBLK - 1) as nb:
                token_major(nb + AT_E2, 0, 0)
            token_major_last(AT_E2 + NBLK - 1, 0, mid_transposes)
            mid_transposes(TT)
            h_split("mid")
            with pe.Fori(AT_O1, AT_O1C) as i:
                feature_major(i)
            for g in range(NG):
                half = 0 if g % 2 else 4
                pe.wait_ge(lo_ready, AT_O1C * SLOTS + g + 1)
                for k in range(4):
                    pe.wait_ge(pool_lo_ready, 4 * g + k + 1)
                    for m in range(4):
                        b = half + m
                        if k == 0:
                            used = uses4(b, "map", g // 2) if half else AT_O1C + g // 2
                            pe.wait_ge(bank_free[b], used + 1)
                        w = (w_hi[:, g, k * T + m * P:k * T + (m + 1) * P],
                             w_lo[:, g, k * T + m * P:k * T + (m + 1) * P])
                        last = product(bank[b][:, :], w, operand(4 * g + k), k == 0, k == 3)
                last.then_inc(slab_done, 1)
            with pe.Fori(0, NBLK - 1) as nb:
                token_major(nb + AT_O2, 1, KT)
            token_major_last(AT_O2 + NBLK - 1, 1, lambda t: None)

        @block.scalar
        def _(act):
            for t in range(TT):
                act.dma_start(tok[:, t, :], x[t * P:(t + 1) * P, :]).then_inc(x_loaded[t], 16)

            def split(slot, n, turn):
                act.wait_ge(raw_loaded[slot % RAW], turn * 16 + 16)
                act.wait_ge(slab_done, done(n - SLOTS) + 1)
                nc.scalar.activation(w_hi[:, slot, :], raw[:, slot % RAW, :], ACT.Copy)\
                    .then_inc(hi_ready, 1)

            def split_ahead(step, q):
                a = q + LOOKAHEAD
                split(a % SLOTS, step * SLOTS + a, step * (SLOTS // RAW) + a // RAW)

            def squares(src, n, by):
                for j in range(4):
                    by(j)
                    count = 4 * TILES_SQUARED.index(n) + j
                    if count >= 2:
                        act.wait_ge(squared, count - 1)
                    nc.scalar.activation(junk[:, j % 2, :], part4(src, j), ACT.Square,
                                         accum_out=sumsq[:, n, j:j + 1]).then_inc(squared, 1)

            def h_rounded(n, t):
                for j in range(4):
                    act.wait_ge(transposed, 4 * n + j + 1)
                    nc.scalar.activation(
                        h_hi[:, 4 * j:4 * j + 4, t * P:(t + 1) * P],
                        bank[4 + j][:, :].rearrange("p (k c) -> p k c", c=P), ACT.Copy)\
                        .then_inc(h_hi_ready, 1)

            for t in range(TT):
                act.wait_ge(x_loaded[t], 16)
                squares(tok[:, t, :], PRE0 + t, lambda j: None)
                if t > 0:
                    h_rounded(t - 1, t - 1)
            split(0, 0, 0)
            h_rounded(TT - 1, TT - 1)
            split(1, 1, 0)
            split(2, 2, 1)

            act.wait_ge(vec_loaded, 16)
            with act.Fori(0, E1A) as c:
                split_ahead(c, 0)
                act.wait_ge(slab_done, done(c * SLOTS + 1))
                act.wait_ge(bank_free[1], c + 1)
                nc.scalar.activation(sig, bank[0][:, :], ACT.Sigmoid).then_inc(bank_free[0], 1)
                split_ahead(c, 1)
                act.wait_ge(bank_free[1], c + 2)
                nc.scalar.activation(tile(c + CB), glu[:, PAD - CONV_B + 1:PAD - CONV_B + 1 + T],
                                     ACT.Identity, bias=col("bias_b", c),
                                     scale=tap("conv_b", c, CONV_B, 0)).then_inc(seeded_b, 1)
                split_ahead(c, 2)
                act.wait_ge(slab_done, done(c * SLOTS + 3))
                act.wait_ge(bank_free[3], c + 1)
                nc.scalar.activation(a_c, bank[2][:, :], ACT.Copy).then_inc(bank_free[2], 1)
                split_ahead(c, 3)
                act.wait_ge(bank_free[3], c + 2)
                nc.scalar.activation(tile(c), prod[:, PAD - CONV_A + 1:PAD - CONV_A + 1 + T],
                                     ACT.Identity, bias=0.0,
                                     scale=tap("conv_a", c, CONV_A, 0)).then_inc(seeded_a, 1)

            def gate(q, step, n, buf):
                act.wait_ge(slab_done, done(step * SLOTS + (q + 1)))
                act.wait_ge(gated, n + 1)
                nc.scalar.activation(sz[buf], bank[q][:, :], ACT.Silu)\
                    .then_inc(bank_free[q], 1)

            def e1b(i):
                split_ahead(i + E1A, 0)
                split_ahead(i + E1A, 1)
                gate(1, i + E1A, i * 2, 0)
                split_ahead(i + E1A, 2)
                split_ahead(i + E1A, 3)
                gate(3, i + E1A, i * 2 + 1, 1)

            e1b(0)
            act.wait_ge(stat_ready, 1)
            nc.scalar.activation(mean, bank[4][:, :], ACT.Copy, scale=1.0 / W_A)\
                .then_inc(bank_free[4], 1)
            with act.Fori(1, E1B) as i:
                e1b(i)
            with act.Fori(0, E1C) as i:
                for q in range(SLOTS):
                    split_ahead(i + (E1A + E1B), q)
                    gate(q, i + (E1A + E1B), i * 4 + (CB + q), q % 2)
                    c = i * 4 + q
                    act.wait_ge(ln_scaled, c + 1)
                    nc.scalar.activation(tile(c + CB), tile(c + CB), ACT.Silu,
                                         bias=col("ln_b", c), scale=col("ln_g", c))\
                        .then_inc(ln_silu, 1)

            act.wait_ge(slab_done, done(E1 * SLOTS))
            for k in range(KT):
                act.wait_ge(gated, 2 + k + 1)
                nc.scalar.activation(h_hi[:, k, :], rows[:, k, :], ACT.Copy)\
                    .then_inc(u_hi_ready, 1)

            def y_squares(t, step, first, layer, sets, nb):
                if t < TT - 1:
                    act.wait_ge(acc_ready, first * (TT - 1) + (layer * NBLK * (TT - 1) + t + 1))
                else:
                    act.wait_ge(slab_done, done(step * SLOTS + SLOTS))
                nc.scalar.activation(junk_y[t], bank[t][:, :], ACT.Square,
                                     accum_out=sumsq[:, sets[t], bass.ds(nb, 1)])\
                    .then_inc(y_squared, 1)

            def blocks(at, layer, sets):
                with act.Fori(0, NBLK - 1) as nb:
                    for q in range(SLOTS):
                        split_ahead(nb + at, q)
                    for t in range(TT):
                        y_squares(t, nb + at, nb, layer, sets, nb)
                split_ahead(at + NBLK - 1, 0)

            mid_sets = [MID + 2 * t for t in range(TT)]
            blocks(AT_E2, 0, mid_sets)
            end = AT_E2 + NBLK - 1

            def mid_norm(t):
                y_squares(t, end, NBLK - 1, 0, mid_sets, NBLK - 1)
                squares(tok[:, t, :], MID + 2 * t + 1,
                        lambda j: act.wait_ge(x_mid_ready, 4 * t + j + 1))
                act.dma_start(x_mid[t * P:(t + 1) * P, :], tok[:, t, :]).then_inc(mid_stored, 16)

            def mid_rounded(t):
                h_rounded(TT + t, t)
                if t + 2 < TT:
                    act.dma_start(resid[t % 2], x[(t + 2) * P:(t + 3) * P, :])\
                        .then_inc(resid_loaded[t % 2], 16)

            mid_norm(0)
            mid_norm(1)
            mid_rounded(0)
            mid_norm(2)
            mid_rounded(1)
            split_ahead(end, 1)
            split_ahead(end, 2)
            mid_norm(3)
            mid_rounded(2)
            mid_rounded(3)
            split_ahead(end, 3)

            with act.Fori(0, O1V) as g:
                for q in range(SLOTS):
                    split_ahead(g + AT_O1, q)
                    act.wait_ge(slab_done, done(g * SLOTS + (AT_O1 * SLOTS + q + 1)))
                    act.wait_ge(v_used, g * 4 + (q + 1))
                    nc.scalar.activation(v_row[:, PAD:], bank[q][:, :], ACT.Copy)\
                        .then_inc(bank_free[q], 1)
            with act.Fori(0, O1Z) as g:
                for q in range(SLOTS):
                    split_ahead(g + (AT_O1 + O1V), q)
                    act.wait_ge(slab_done, done(g * SLOTS + ((AT_O1 + O1V) * SLOTS + q + 1)))
                    nc.scalar.activation(silu_z[:, bass.ds(g * 4 + q, 1), :].rearrange("p a t -> p (a t)"),
                                         bank[q][:, :], ACT.Silu).then_inc(bank_free[q], 1)

            def u_rounded(g):
                for m in range(4):
                    j = 4 * g + m
                    b = m if g % 2 else 4 + m
                    used = AT_O1C + g // 2 if g % 2 else uses4(b, "map", g // 2)
                    act.wait_ge(bank_free[b], used + 2)
                    nc.scalar.activation(h_hi[:, j, :], rows[:, j, :], ACT.Copy)\
                        .then_inc(u_hi_ready, 1)

            act.wait_ge(slab_done, done(AT_O1C * SLOTS))
            act.wait_ge(v_used, KT + 1)
            for g in range(NG):
                for k in range(4 * g, 4 * g + 4):
                    nc.scalar.activation(h_hi[:, k, :], rows[:, k, :], ACT.Copy)\
                        .then_inc(pool_hi_ready, 1)
                split_ahead(AT_O1C, g)
                if g > 0:
                    u_rounded(g - 1)
            u_rounded(NG - 1)

            post_sets = [POST1 + t for t in range(TT)]
            blocks(AT_O2, 1, post_sets)
            for t in range(TT):
                y_squares(t, AT_O2 + NBLK - 1, NBLK - 1, 1, post_sets, NBLK - 1)
                if t in (1, 2):
                    act.wait_ge(out_ready, 4 * t)
                    act.dma_start(resid[(t + 1) % 2], x_mid[(t + 1) * P:(t + 2) * P, :])\
                        .then_inc(resid_loaded[(t + 1) % 2], 16)

        @block.vector
        def _(dve):
            chain = [0, 0]

            def link(ins):
                chain[0] += 1
                ins.then_inc(dve_done, 1)
                dve.wait_ge(dve_done, chain[1] + chain[0])

            def split(slot, n):
                dve.wait_ge(hi_ready, n + 1)
                nc.vector.tensor_tensor(w_lo[:, slot, :], raw[:, slot % RAW, :],
                                        f32(w_hi[:, slot, :]), ALU.subtract)\
                    .then_inc(lo_ready, 1)

            def split_ahead(step, q):
                a = q + LOOKAHEAD
                split(a % SLOTS, step * SLOTS + a)

            def mean_square(n):
                link(nc.vector.reduce_sum(total[:, n:n + 1], sumsq[:, n, :], AX.X))
                nc.vector.tensor_scalar(meansq[:, n:n + 1], total[:, n:n + 1], 1.0 / D, EPS,
                                        ALU.mult, ALU.add).then_inc(mean_squared, 1)

            def scaled(dst, src, n, gain):
                dve.wait_ge(rstd_ready, n + 1)
                for j in range(4):
                    nc.vector.scalar_tensor_tensor(
                        out=part4(dst, j), in0=part4(src, j), scalar=rstd[:, n:n + 1],
                        in1=part4(gain, j), op0=ALU.mult, op1=ALU.mult).then_inc(normed, 1)

            def h_rest(n, t):
                for j in range(4):
                    dve.wait_ge(h_hi_ready, 4 * n + j + 1)
                    at = (slice(None), slice(4 * j, 4 * j + 4), slice(t * P, (t + 1) * P))
                    nc.vector.tensor_tensor(
                        h_lo[at], bank[4 + j][:, :].rearrange("p (k c) -> p k c", c=P),
                        f32(h_hi[at]), ALU.subtract).then_inc(bank_free[4 + j], 1)

            dve.wait_ge(gain_pre_loaded, 16)
            for t in range(TT):
                dve.wait_ge(squared, 4 * t + 4)
                mean_square(PRE0 + t)
                scaled(tok[:, t, :], tok[:, t, :], PRE0 + t, gain_pre)
                if t > 0:
                    h_rest(t - 1, t - 1)
            split(0, 0)
            h_rest(TT - 1, TT - 1)
            split(1, 1)
            split(2, 2)

            def convolve(c, taps, row, width, name, first, last):
                dst = tile(c + CB) if name == "conv_b" else tile(c)
                for j in range(first, last):
                    at = PAD - width + 1 + j
                    ins = nc.vector.scalar_tensor_tensor(
                        out=dst, in0=row[:, at:at + T], scalar=tap(name, c, width, j), in1=dst,
                        op0=ALU.mult, op1=ALU.add)
                    if taps is not None and j == width - 1:
                        ins.then_inc(taps, 1)
                    else:
                        link(ins)

            dve.wait_ge(vec_loaded, 16)
            dve.wait_ge(consts_set, 6)
            before, links = chain[0], CONV_B - 2 + CONV_A - 1
            with dve.Fori(0, E1A) as c:
                chain[1] = c * links
                split_ahead(c, 0)
                split_ahead(c, 1)
                dve.wait_ge(slab_done, done(c * SLOTS + 2))
                dve.wait_ge(bank_free[0], c + 2)
                nc.vector.tensor_tensor(glu[:, PAD:], bank[1][:, :], sig, ALU.mult)\
                    .then_inc(bank_free[1], 1)
                dve.wait_ge(bank_free[1], c + 2)
                dve.wait_ge(seeded_b, c + 1)
                convolve(c, conv_done, glu, CONV_B, "conv_b", 1, 11)
                split_ahead(c, 2)
                convolve(c, conv_done, glu, CONV_B, "conv_b", 11, 21)
                split_ahead(c, 3)
                dve.wait_ge(slab_done, done(c * SLOTS + 4))
                dve.wait_ge(bank_free[2], c + 2)
                nc.vector.tensor_tensor(prod[:, PAD:], bank[3][:, :], a_c, ALU.mult)\
                    .then_inc(bank_free[3], 1)
                convolve(c, conv_done, glu, CONV_B, "conv_b", 21, CONV_B)
                dve.wait_ge(bank_free[3], c + 2)
                dve.wait_ge(seeded_a, c + 1)
                convolve(c, None, prod, CONV_A, "conv_a", 1, CONV_A)
            assert chain[0] == before + links
            chain[:] = before + links * E1A, 0

            def e1b(i):
                step = i + E1A
                for q in range(SLOTS):
                    c = i * 2 + q // 2
                    split_ahead(step, q)
                    if q % 2 == 0:
                        dve.wait_ge(slab_done, done(step * SLOTS + (q + 1)))
                        nc.vector.tensor_tensor(tile(c), tile(c), bank[q][:, :], ALU.mult)\
                            .then_inc(bank_free[q], 1)
                    else:
                        dve.wait_ge(bank_free[q - 1], step + 2)
                        dve.wait_ge(bank_free[q], step + 2)
                        nc.vector.tensor_tensor(tile(c), tile(c), sz[q // 2], ALU.mult)\
                            .then_inc(gated, 1)

            with dve.Fori(0, E1B - 1) as i:
                e1b(i)
            dve.wait_ge(stat_ready, 2)
            nc.vector.tensor_scalar(var, bank[5][:, :], 1.0 / W_A, EPS, ALU.mult, ALU.add)\
                .then_inc(bank_free[5], 1)
            e1b(E1B - 1)

            dve.wait_ge(ln_rstd_ready, 1)
            with dve.Fori(0, E1C) as i:
                for q in range(SLOTS):
                    c = i * 4 + q
                    nc.vector.tensor_tensor(tile(c + CB), tile(c + CB), ln_rstd, ALU.mult)\
                        .then_inc(ln_scaled, 1)
                    split_ahead(i + (E1A + E1B), q)
                    dve.wait_ge(ln_silu, c + 1)
                    dve.wait_ge(bank_free[q], i + (E1A + E1B + 2))
                    nc.vector.tensor_tensor(tile(c + CB), tile(c + CB), sz[q % 2], ALU.mult)\
                        .then_inc(gated, 1)

            def u_rest(j, n):
                dve.wait_ge(u_hi_ready, n + 1)
                nc.vector.tensor_tensor(h_lo[:, j, :], rows[:, j, :], f32(h_hi[:, j, :]),
                                        ALU.subtract).then_inc(u_lo_ready, 1)

            for k in range(KT):
                u_rest(k, k)

            def y_gained(t, nb, count):
                dve.wait_ge(y_squared, count + (t + 1))
                nc.vector.tensor_tensor(tok[:, t, bass.ds(nb * T, T)], bank[t][:, :],
                                        gain_post[:, bass.ds(nb * T, T)], ALU.mult)\
                    .then_inc(bank_free[t], 1)

            def blocks(at, layer):
                with dve.Fori(0, NBLK - 1) as nb:
                    for q in range(SLOTS):
                        split_ahead(nb + at, q)
                    for t in range(TT):
                        y_gained(t, nb, nb * TT + layer * NBLK * TT)
                split_ahead(at + NBLK - 1, 0)

            def added(t, n, layer, used, ready):
                y_gained(t, NBLK - 1, (layer * NBLK + NBLK - 1) * TT)
                mean_square(n)
                dve.wait_ge(bank_free[t], used + 2)
                dve.wait_ge(rstd_ready, n + 1)
                dve.wait_ge(resid_loaded[t % 2], 16 * (2 * layer + t // 2 + 1))
                for j in range(4):
                    nc.vector.scalar_tensor_tensor(
                        out=part4(tok[:, t, :], j), in0=part4(tok[:, t, :], j),
                        scalar=rstd[:, n:n + 1], in1=part4(resid[t % 2], j),
                        op0=ALU.mult, op1=ALU.add).then_inc(ready, 1)

            dve.wait_ge(gain_end_loaded, 32)
            blocks(AT_E2, 0)
            end = AT_E2 + NBLK - 1

            def mid_norm(t):
                added(t, MID + 2 * t, 0, end, x_mid_ready)
                dve.wait_ge(squared, 4 * (TT + t) + 4)
                mean_square(MID + 2 * t + 1)
                scaled(resid[t % 2], tok[:, t, :], MID + 2 * t + 1, gain_next)

            mid_norm(0)
            mid_norm(1)
            h_rest(TT + 0, 0)
            mid_norm(2)
            h_rest(TT + 1, 1)
            split_ahead(end, 1)
            split_ahead(end, 2)
            mid_norm(3)
            h_rest(TT + 2, 2)
            h_rest(TT + 3, 3)
            split_ahead(end, 3)

            dve.wait_ge(mid_stored, 16 * TT)
            for g, window in enumerate(WINDOWS):
                for q in range(SLOTS):
                    j = 4 * g + q
                    split_ahead(AT_O1 + g, q)
                    dve.wait_ge(bank_free[q], AT_O1 + g + 2)
                    src, step = v_row, 1
                    while step < window:
                        dst = sum_a if src is not sum_a else sum_b
                        link(nc.vector.tensor_tensor(
                            dst[:, PAD:], src[:, PAD:], src[:, PAD - step:PAD - step + T],
                            ALU.add))
                        src, step = dst, 2 * step
                    start = src[:, PAD:PAD + window]
                    rest = slice(PAD + window, PAD + T)
                    nc.vector.scalar_tensor_tensor(
                        out=rows[:, j, window:], in0=src[:, rest], scalar=1.0 / window,
                        in1=v_row[:, rest], op0=ALU.mult, op1=ALU.subtract)
                    link(nc.vector.tensor_tensor(start, start, inv_count[:, 0:window],
                                                       ALU.mult))
                    nc.vector.tensor_tensor(rows[:, j, 0:window], start,
                                            v_row[:, PAD:PAD + window], ALU.subtract)\
                        .then_inc(v_used, 1)
            with dve.Fori(0, O1Z) as g:
                for q in range(SLOTS):
                    split_ahead(g + (AT_O1 + O1V), q)
                    dve.wait_ge(bank_free[q], g + (AT_O1 + O1V + 2))
                    z = silu_z[:, bass.ds(g * 4 + q, 1), :].rearrange("p a t -> p (a t)")
                    nc.vector.tensor_scalar(z, z, col("c_scale", g * 4 + q), None, ALU.mult)\
                        .then_inc(z_scaled, 1)

            def group(g):
                dve.wait_ge(slab_done, done(AT_O1C * SLOTS + g + 1))
                for m in range(4):
                    j, b = 4 * g + m, (m if g % 2 else 4 + m)
                    nc.vector.scalar_tensor_tensor(
                        out=rows[:, j, :], in0=bank[b][:, :], scalar=col("c_b", j),
                        in1=silu_z[:, j, :], op0=ALU.add, op1=ALU.mult)\
                        .then_inc(bank_free[b], 1)
                for j in range(4 * g, 4 * g + 4):
                    u_rest(j, KT + j)

            dve.wait_ge(z_scaled, KT)
            for g in range(NG):
                split_ahead(AT_O1C, g)
                if g > 0:
                    group(g - 1)
            group(NG - 1)

            dve.wait_ge(gain_end_loaded, 48)
            blocks(AT_O2, 1)
            for t in range(TT):
                added(t, POST1 + t, 1, AT_O2 + NBLK, out_ready)


def kernel(**inputs):
    import concourse.bacc as bacc
    from concourse.bass_utils import run_bass_kernel_spmd

    conv_b = np.asarray(inputs["e_b_conv"]).reshape(CONV_B, CB, P).transpose(2, 1, 0)
    conv_a = np.asarray(inputs["e_a_conv"]).reshape(CONV_A, CB, P).transpose(2, 1, 0)
    packed = [conv_b.reshape(P, -1), conv_a.reshape(P, -1)]
    for name, tiles in (("e_b_conv_bias", CB), ("e_b_ln_g", CB), ("e_b_ln_b", CB),
                        ("o_c_b", KT), ("o_c_scale", KT)):
        packed.append(np.asarray(inputs[name]).reshape(tiles, P).T)
    arrays = {
        "x": np.asarray(inputs["x"]).reshape(T, D),
        "vec": np.concatenate(packed, axis=1),
        "e_pre": np.asarray(inputs["e_norm_pre"]),
        "e_post": np.asarray(inputs["e_norm_post"]),
        "e_in": np.asarray(inputs["e_w_in"])[0],
        "e_out": np.asarray(inputs["e_w_out"])[0],
        "o_pre": np.asarray(inputs["o_norm_pre"]),
        "o_post": np.asarray(inputs["o_norm_post"]),
        "o_in": np.asarray(inputs["o_w_in"])[0],
        "o_cw": np.asarray(inputs["o_c_w"])[0],
        "o_out": np.asarray(inputs["o_w_out"])[0],
    }
    arrays = {name: np.ascontiguousarray(a) for name, a in arrays.items()}
    nc = bacc.Bacc("TRN2", target_bir_lowering=False, num_devices=1,
                   dynamic_dma_scratch_size=1024)
    aps = [nc.dram_tensor(name, a.shape, F32, kind="ExternalInput").ap()
           for name, a in arrays.items()]
    result = nc.dram_tensor("out", (T, D), F32, kind="ExternalOutput").ap()
    build(nc, *aps, result)
    got = run_bass_kernel_spmd(nc, [arrays], core_ids=[0]).results[0]["out"]
    return got.reshape(inputs["x"].shape)
```

```python
from contextlib import ExitStack

import numpy as np

import concourse.bass as bass
from concourse import mybir

F32 = mybir.dt.float32
F32R = mybir.dt.float32r
BF16 = mybir.dt.bfloat16
ALU = mybir.AluOpType
ACT = mybir.ActivationFunctionType
AX = mybir.AxisListType

P = 128
D = 2048
T = 512
TT = T // P
KT = D // P
QUARTER = KT // 4
W_A = D // 2
CB = W_A // P
CONV_A, CONV_B = 3, 31
WINDOWS = (2, 4, 8, 16)
NG = len(WINDOWS)
G_C = D // NG
EPS = 1e-6

SLAB = 2048
SLOTS = 4
RAW = 2
LOOKAHEAD = SLOTS - 1
NBLK = D // T
PAD = 32

E1A = CB
E1B = CB // 2
E1C = CB // 4
E1 = E1A + E1B + E1C
E2 = NBLK
O1V = O1Z = KT // 4
O1C = 1
O2 = NBLK
AT_E2 = E1
AT_O1 = AT_E2 + E2
AT_O1C = AT_O1 + O1V + O1Z
AT_O2 = AT_O1C + O1C
STEPS = AT_O2 + O2
LAST = SLOTS * STEPS

A_X, A_B, A_C, A_Z, B_VAL, B_GATE, B_Z = (n * W_A for n in range(7))

PRE0 = 0
MID = TT
POST1 = 3 * TT
SETS = 4 * TT
TILES_SQUARED = [PRE0 + t for t in range(TT)] + [MID + 2 * t + 1 for t in range(TT)]

VECTORS = (("conv_b", CB * CONV_B), ("conv_a", CB * CONV_A), ("bias_b", CB), ("ln_g", CB),
           ("ln_b", CB), ("c_b", KT), ("c_scale", KT))
AT_VEC = {name: sum(n for _, n in VECTORS[:i]) for i, (name, _) in enumerate(VECTORS)}
NVEC = sum(n for _, n in VECTORS)


def build(nc, x, vec, e_pre, e_post, e_in, e_out, o_pre, o_post, o_in, o_cw, o_out, out):
    ctx = ExitStack()
    with ctx:
        def sb(name, shape, dt=F32):
            return ctx.enter_context(nc.sbuf_tensor(name, shape, dt))

        def sem(name):
            return ctx.enter_context(nc.semaphore(name))

        h_hi = sb("h_hi", [P, KT, T], F32R)
        h_lo = sb("h_lo", [P, KT, T], F32R)
        rows = sb("rows", [P, KT, T])
        tok = rows[:, :, :].rearrange("p (t a) c -> p t (a c)", t=TT)
        raw = sb("raw", [P, RAW, SLAB])
        w_hi = sb("w_hi", [P, SLOTS, SLAB], F32R)
        w_lo = sb("w_lo", [P, SLOTS, SLAB], F32R)
        scratch = sb("scratch", [P, KT * T])
        shifted = sb("shifted", [P, 3, PAD + T])
        vecs = sb("vecs", [P, NVEC])
        ident = sb("ident", [P, P])
        ones = sb("ones", [P, P])
        inv_count = sb("inv_count", [P, WINDOWS[-1]])
        minus_half = sb("minus_half", [P, 1])
        junk = sb("junk", [P, 2, T], BF16)
        sumsq = sb("sumsq", [P, SETS, NBLK])
        total = sb("total", [P, SETS])
        meansq = sb("meansq", [P, SETS])
        rstd = sb("rstd", [P, SETS])
        ln_var = sb("ln_var", [P, TT])
        ln_power = sb("ln_power", [P, TT])
        diagonals = sb("diagonals", [P, TT, P])

        gain_pre = scratch[:, 0:D]
        sig, a_c, csum, mean, vsum, ln_rstd, sq, sz0, sz1 = (
            scratch[:, D + n * T:D + (n + 1) * T] for n in range(9))
        sz = (sz0, sz1)
        gain_post, gain_next, resid0, resid1 = (scratch[:, n * D:(n + 1) * D] for n in range(4))
        resid = (resid0, resid1)
        silu_z = scratch[:, :].rearrange("p (j t) -> p j t", j=KT)

        glu, prod = shifted[:, 0, :], shifted[:, 1, :]
        v_row, sum_a, sum_b = (shifted[:, n, :] for n in range(3))
        junk_y = [shifted[:, t // 2, PAD:].bitcast(BF16)[:, t % 2 * T:(t % 2 + 1) * T]
                  for t in range(TT)]

        bank = [ctx.enter_context(nc.psum_tensor(f"bank{b}", [P, T], F32)) for b in range(8)]

        x_mid = nc.dram_tensor("x_mid", [T, D], F32, kind="Internal").ap()

        x_loaded = [sem(f"x_loaded{t}") for t in range(TT)]
        vec_loaded = sem("vec_loaded")
        gain_pre_loaded = [sem(f"gain_pre_loaded{j}") for j in range(4)]
        gain_end_loaded = sem("gain_end_loaded")
        resid_loaded = [sem(f"resid_loaded{s}") for s in range(2)]
        mid_stored = sem("mid_stored")
        out_stored = sem("out_stored")
        consts_set = sem("consts_set")
        pool_done = sem("pool_done")
        raw_loaded = [sem(f"raw_loaded{s}") for s in range(RAW)]
        hi_ready = sem("hi_ready")
        lo_ready = sem("lo_ready")
        slab_done = sem("slab_done")
        h_used = sem("h_used")
        acc_ready = sem("acc_ready")
        bank_free = [sem(f"bank_free{b}") for b in range(8)]
        transposed = sem("transposed")
        stat_ready = sem("stat_ready")
        squared = sem("squared")
        mean_squared = sem("mean_squared")
        rstd_ready = sem("rstd_ready")
        normed = sem("normed")
        h_hi_ready = sem("h_hi_ready")
        dve_done = sem("dve_done")
        seeded_b = sem("seeded_b")
        seeded_a = sem("seeded_a")
        conv_done = sem("conv_done")
        csum_ready = sem("csum_ready")
        vsum_ready = sem("vsum_ready")
        ln_rstd_ready = sem("ln_rstd_ready")
        diagonals_ready = sem("diagonals_ready")
        ln_scaled = sem("ln_scaled")
        ln_silu = sem("ln_silu")
        gated = sem("gated")
        u_hi_ready = sem("u_hi_ready")
        u_lo_ready = sem("u_lo_ready")
        y_squared = sem("y_squared")
        x_mid_ready = sem("x_mid_ready")
        z_scaled = sem("z_scaled")
        v_used = sem("v_used")
        pool_hi_ready = sem("pool_hi_ready")
        pool_lo_ready = sem("pool_lo_ready")
        out_ready = sem("out_ready")

        def f32(ap):
            return ap.bitcast(F32)

        def col(name, n, step=1):
            return vecs[:, bass.ds(n * step + AT_VEC[name], 1)]

        def tap(name, c, taps, j):
            return vecs[:, bass.ds(c * taps + (AT_VEC[name] + j), 1)]

        def tile(n):
            if isinstance(n, int):
                return rows[:, n, :]
            return rows[:, bass.ds(n, 1), :].rearrange("p a t -> p (a t)")

        def done(n):
            return n + SLOTS

        def uses4(b, part, n=0):
            stat = 1 if b < 7 else 0
            return {"start": 0, "stat": TT, "mid": TT + stat, "map": 2 * TT + stat}[part] + n

        def part4(ap, j):
            return ap[:, j * T:(j + 1) * T]

        block = ctx.enter_context(nc.Block())

        @block.sync
        def _(sp):
            def load_x(t):
                sp.dma_start(tok[:, t, :], x[t * P:(t + 1) * P, :]).then_inc(x_loaded[t], 16)

            load_x(0)
            load_x(1)
            for j in range(4):
                sp.dma_start(part4(gain_pre, j), e_pre[:, j * T:(j + 1) * T].to_broadcast([P, T]))\
                    .then_inc(gain_pre_loaded[j], 16)

            def load(slot, src, n=None):
                if n is not None:
                    sp.wait_ge(lo_ready, n - (RAW - 1))
                dst = raw[:, slot % RAW, :].rearrange("p (k c) -> p k c", c=src.shape[-1])
                sp.dma_start(dst, src).then_inc(raw_loaded[slot % RAW], 16)

            def columns(w, first):
                return w.rearrange("(k p) n -> p k n", p=P)[:, :, bass.ds(first, P)]

            def block_part(w, nb, q):
                v = w.rearrange("(k p) n -> p k n", p=P)
                return v[:, q * KT // 4:(q + 1) * KT // 4, bass.ds(nb * T, T)]

            E1A_ORDER = (B_GATE, B_VAL, A_C, A_X)
            for q, kind in enumerate(E1A_ORDER):
                load(q, columns(e_in, kind), q if q >= RAW else None)
                if q == RAW - 1:
                    load_x(2)
                    load_x(3)
                    sp.dma_start(vecs[:, :], vec).then_inc(vec_loaded, 16)
            with sp.Fori(0, E1A - 1) as i:
                for q, kind in enumerate(E1A_ORDER):
                    load(q, columns(e_in, i * P + (P + kind)), i * SLOTS + (SLOTS + q))
            with sp.Fori(0, E1B) as i:
                for q, kind in enumerate((A_B, A_Z, A_B + P, A_Z + P)):
                    load(q, columns(e_in, i * (2 * P) + kind), i * SLOTS + (E1A * SLOTS + q))
            with sp.Fori(0, E1C) as i:
                for q in range(SLOTS):
                    load(q, columns(e_in, i * (4 * P) + (B_Z + q * P)),
                         i * SLOTS + ((E1A + E1B) * SLOTS + q))

            def token_major_loads(w, step, gains, rows_in, u_tiles):
                for q in range(SLOTS):
                    load(q, block_part(w, 0, q), step * SLOTS + q)
                sp.wait_ge(u_lo_ready, u_tiles)
                for dst, src in gains:
                    sp.dma_start(dst, src.to_broadcast([P, D])).then_inc(gain_end_loaded, 16)
                for t in range(2):
                    sp.dma_start(resid[t], rows_in[t * P:(t + 1) * P, :])\
                        .then_inc(resid_loaded[t], 16)
                with sp.Fori(1, NBLK) as nb:
                    for q in range(SLOTS):
                        load(q, block_part(w, nb, q), nb * SLOTS + (step * SLOTS + q))

            token_major_loads(e_out, AT_E2, ((gain_post, e_post), (gain_next, o_pre)), x, KT)
            with sp.Fori(0, O1V + O1Z) as g:
                for q in range(SLOTS):
                    load(q, columns(o_in, g * (4 * P) + q * P), g * SLOTS + (AT_O1 * SLOTS + q))
            for g in range(NG):
                load(g, o_cw[g].rearrange("(k p) n -> p k n", p=P), AT_O1C * SLOTS + g)
            token_major_loads(o_out, AT_O2, ((gain_post, o_post),), x_mid, 2 * KT)
            for t in range(TT - 1):
                sp.wait_ge(out_ready, 4 * t + 4)
                sp.dma_start(out[t * P:(t + 1) * P, :], tok[:, t, :]).then_inc(out_stored, 16)
            for j in range(4):
                sp.wait_ge(out_ready, 4 * (TT - 1) + j + 1)
                sp.dma_start(out[(TT - 1) * P:, j * T:(j + 1) * T],
                             part4(tok[:, TT - 1, :], j)).then_inc(out_stored, 16)
            sp.wait_ge(out_stored, 16 * (TT - 1 + 4))

        @block.gpsimd
        def _(pool):
            for b in range(8):
                pool.sem_inc(bank_free[b], 1)
            pool.sem_inc(gated, 2)
            pool.sem_inc(v_used, 1)
            nc.gpsimd.memset(ident[:, :], 0.0).then_inc(pool_done, 1)
            pool.wait_ge(pool_done, 1)
            nc.gpsimd.affine_select(out=ident[:, :], in_=ident[:, :], compare_op=ALU.not_equal,
                                    fill=1.0, base=0, pattern=[[-1, P]],
                                    channel_multiplier=1).then_inc(consts_set, 1)
            nc.gpsimd.memset(minus_half[:, :], -0.5).then_inc(consts_set, 1)
            nc.gpsimd.memset(ones[:, :], 1.0).then_inc(consts_set, 1)
            nc.gpsimd.memset(shifted[:, :, 0:PAD], 0.0).then_inc(consts_set, 1)
            nc.gpsimd.memset(csum, 0.0).then_inc(consts_set, 1)
            nc.gpsimd.memset(vsum, 0.0).then_inc(consts_set, 1)
            for n in range(WINDOWS[-1]):
                nc.gpsimd.memset(inv_count[:, n:n + 1], 1.0 / (n + 1)).then_inc(consts_set, 1)
            pool.wait_ge(consts_set, 6)

            def powers(first, count):
                for n in range(first, first + count):
                    pool.wait_ge(mean_squared, n + 1)
                    nc.gpsimd.tensor_tensor(rstd[:, n:n + 1], meansq[:, n:n + 1],
                                            minus_half[:, :], ALU.pow).then_inc(rstd_ready, 1)

            powers(PRE0, TT)

            for c in range(CB):
                pool.wait_ge(conv_done, c + 1)
                nc.gpsimd.tensor_tensor(csum, csum, tile(c + CB), ALU.add)\
                    .then_inc(csum_ready, 1)
                pool.wait_ge(csum_ready, c + 1)

            pool.wait_ge(bank_free[4], uses4(4, "stat") + 2)
            for c in range(CB):
                nc.gpsimd.tensor_tensor(tile(c + CB), tile(c + CB), mean, ALU.subtract)\
                    .then_inc(pool_done, 1)
                pool.wait_ge(pool_done, c * 2 + 2)
                nc.gpsimd.tensor_tensor(sq, tile(c + CB), tile(c + CB), ALU.mult)\
                    .then_inc(pool_done, 1)
                pool.wait_ge(pool_done, c * 2 + 3)
                nc.gpsimd.tensor_tensor(vsum, vsum, sq, ALU.add).then_inc(vsum_ready, 1)
                pool.wait_ge(vsum_ready, c + 1)

            pool.wait_ge(bank_free[5], uses4(5, "stat") + 2)
            nc.gpsimd.tensor_tensor(ln_power[:, :], ln_var[:, :],
                                    minus_half[:, 0:1].to_broadcast([P, TT]),
                                    ALU.pow).then_inc(ln_rstd_ready, 1)

            powers(MID, 2 * TT)

            for k in range(KT):
                pool.wait_ge(pool_hi_ready, k + 1)
                nc.gpsimd.tensor_tensor(h_lo[:, k, :], rows[:, k, :], f32(h_hi[:, k, :]),
                                        ALU.subtract).then_inc(pool_lo_ready, 1)

            powers(POST1, TT)

        @block.tensor
        def _(pe):
            pe.sem_inc(slab_done, SLOTS)
            pe.wait_ge(consts_set, 3)

            def product(dst, w, m, first, last):
                nc.tensor.matmul(dst, w[0], m[0], start=first, stop=False)
                nc.tensor.matmul(dst, w[0], m[1], start=False, stop=False)
                return nc.tensor.matmul(dst, w[1], m[0], start=False, stop=last)

            def weights(slot, k, width):
                return (w_hi[:, slot, k * width:(k + 1) * width],
                        w_lo[:, slot, k * width:(k + 1) * width])

            def operand(k, first=0, width=T):
                return h_hi[:, k, first:first + width], h_lo[:, k, first:first + width]

            def feature_major(step, last_of_h=False):
                for q in range(SLOTS):
                    pe.wait_ge(lo_ready, step * SLOTS + (q + 1))
                    pe.wait_ge(bank_free[q], step + 1)
                    for k in range(KT):
                        last = product(bank[q][:, :], weights(q, k, P), operand(k),
                                       k == 0, k == KT - 1)
                        if last_of_h and q == SLOTS - 1 and k == QUARTER - 1:
                            last.then_inc(h_used, 1)
                    last.then_inc(slab_done, 1)

            def transposes(part, t, row):
                n = t + (TT if part == "mid" else 0)
                for j in range(4):
                    pe.wait_ge(normed, 4 * n + j + 1)
                    pe.wait_ge(bank_free[4 + j], uses4(4 + j, part, t) + 1)
                    for i in range(4):
                        k = 4 * j + i
                        last = nc.tensor.transpose(bank[4 + j][:, i * P:(i + 1) * P],
                                                   row[:, k * P:(k + 1) * P], ident[:, :])
                    last.then_inc(transposed, 1)

            def halves(step, part, between):
                for half in range(2):
                    tokens = slice(half * T // 2, (half + 1) * T // 2)
                    for q in range(SLOTS):
                        if half == 0:
                            pe.wait_ge(lo_ready, step * SLOTS + q + 1)
                            pe.wait_ge(bank_free[q], step + 1)
                        for k in range(KT):
                            if q == 0 and k % 4 == 0:
                                n = (half + 1) * TT // 2
                                pe.wait_ge(bank_free[4 + k // 4],
                                           uses4(4 + k // 4, part, n) + 1)
                            last = product(bank[q][:, tokens], weights(q, k, P),
                                           operand(k, half * T // 2, T // 2),
                                           k == 0, k == KT - 1)
                        if half == 1:
                            last.then_inc(slab_done, 1)
                        elif q in between:
                            between[q]()

            transposes("start", 0, tok[:, 0, :])
            transposes("start", 1, tok[:, 1, :])
            halves(0, "start", {1: lambda: transposes("start", 2, tok[:, 2, :]),
                                2: lambda: transposes("start", 3, tok[:, 3, :])})
            with pe.Fori(1, E1A + 1) as i:
                feature_major(i)
            pe.wait_ge(csum_ready, CB)
            pe.wait_ge(bank_free[4], uses4(4, "stat") + 1)
            nc.tensor.matmul(bank[4][:, :], ones[:, :], csum, start=True, stop=True)\
                .then_inc(stat_ready, 1)
            with pe.Fori(E1A + 1, E1A + E1B - 1) as i:
                feature_major(i)
            pe.wait_ge(vsum_ready, CB)
            pe.wait_ge(bank_free[5], uses4(5, "stat") + 1)
            for t in range(TT):
                last = nc.tensor.matmul(bank[5][:, t:t + 1], vsum[:, t * P:(t + 1) * P],
                                        ones[:, 0:1], start=True, stop=True)
            last.then_inc(stat_ready, 1)
            feature_major(E1A + E1B - 1)
            pe.wait_ge(diagonals_ready, TT)
            pe.wait_ge(bank_free[6], uses4(6, "stat") + 1)
            nc.tensor.matmul(bank[6][:, :], ones[:, :], diagonals[:, :, :],
                             start=True, stop=True)\
                .then_inc(stat_ready, 1)
            with pe.Fori(E1A + E1B, E1 - 1) as i:
                feature_major(i)
            feature_major(E1 - 1, last_of_h=True)

            def token_major(step, extra, u_first):
                for q in range(SLOTS):
                    pe.wait_ge(lo_ready, step * SLOTS + (q + 1))
                    for kk in range(4):
                        k = 4 * q + kk
                        pe.wait_ge(u_lo_ready, u_first + k + 1)
                        for t in range(TT):
                            if k == 0:
                                pe.wait_ge(bank_free[t], step + (1 + extra))
                            last = product(bank[t][:, :], operand(k, t * P, P),
                                           weights(q, kk, T), k == 0, k == KT - 1)
                            if k == KT - 1 and t < TT - 1:
                                last.then_inc(acc_ready, 1)
                    last.then_inc(slab_done, 1)

            def token_major_last(step, extra, between):
                for t in range(TT):
                    pe.wait_ge(bank_free[t], step + 1 + extra)
                    for q in range(SLOTS):
                        if t == 0:
                            pe.wait_ge(lo_ready, step * SLOTS + q + 1)
                        for kk in range(4):
                            k = 4 * q + kk
                            last = product(bank[t][:, :], operand(k, t * P, P),
                                           weights(q, kk, T), k == 0, k == KT - 1)
                        if t == TT - 1:
                            last.then_inc(slab_done, 1)
                    if t < TT - 1:
                        last.then_inc(acc_ready, 1)
                    between(t)

            def mid_transposes(t):
                if t > 0:
                    transposes("mid", t - 1, resid[(t - 1) % 2])

            with pe.Fori(0, NBLK - 1) as nb:
                token_major(nb + AT_E2, 0, 0)
            token_major_last(AT_E2 + NBLK - 1, 0, mid_transposes)
            halves(AT_O1, "mid", {2: lambda: mid_transposes(TT)})
            with pe.Fori(AT_O1 + 1, AT_O1C - 1) as i:
                feature_major(i)
            feature_major(AT_O1C - 1, last_of_h=True)
            for g in range(NG):
                half = 4 if g % 2 else 0
                pe.wait_ge(lo_ready, AT_O1C * SLOTS + g + 1)
                for k in range(4):
                    pe.wait_ge(pool_lo_ready, 4 * g + k + 1)
                    for m in range(4):
                        b = half + m
                        if k == 0:
                            used = uses4(b, "map", g // 2) if half else AT_O1C + g // 2
                            pe.wait_ge(bank_free[b], used + 1)
                        w = (w_hi[:, g, k * T + m * P:k * T + (m + 1) * P],
                             w_lo[:, g, k * T + m * P:k * T + (m + 1) * P])
                        last = product(bank[b][:, :], w, operand(4 * g + k), k == 0, k == 3)
                last.then_inc(slab_done, 1)
            with pe.Fori(0, NBLK - 1) as nb:
                token_major(nb + AT_O2, 1, KT)
            token_major_last(AT_O2 + NBLK - 1, 1, lambda t: None)

        @block.scalar
        def _(act):
            def split(slot, n, turn):
                act.wait_ge(raw_loaded[slot % RAW], turn * 16 + 16)
                act.wait_ge(slab_done, done(n - SLOTS) + 1)
                nc.scalar.activation(w_hi[:, slot, :], raw[:, slot % RAW, :], ACT.Copy)\
                    .then_inc(hi_ready, 1)

            def split_ahead(step, q):
                a = q + LOOKAHEAD
                split(a % SLOTS, step * SLOTS + a, step * (SLOTS // RAW) + a // RAW)

            def squares(src, n, by):
                for j in range(4):
                    by(j)
                    count = 4 * TILES_SQUARED.index(n) + j
                    if count >= 2:
                        act.wait_ge(squared, count - 1)
                    nc.scalar.activation(junk[:, j % 2, :], part4(src, j), ACT.Square,
                                         accum_out=sumsq[:, n, j:j + 1]).then_inc(squared, 1)

            def h_rounded(n, t):
                for j in range(4):
                    act.wait_ge(transposed, 4 * n + j + 1)
                    nc.scalar.activation(
                        h_hi[:, 4 * j:4 * j + 4, t * P:(t + 1) * P],
                        bank[4 + j][:, :].rearrange("p (k c) -> p k c", c=P), ACT.Copy)\
                        .then_inc(h_hi_ready, 1)

            def x_squares(t):
                act.wait_ge(x_loaded[t], 16)
                squares(tok[:, t, :], PRE0 + t, lambda j: None)

            x_squares(0)
            x_squares(1)
            h_rounded(0, 0)
            split(0, 0, 0)
            h_rounded(1, 1)
            split(1, 1, 0)
            x_squares(2)
            split(2, 2, 1)
            x_squares(3)
            h_rounded(2, 2)
            split_ahead(0, 0)
            h_rounded(3, 3)

            act.wait_ge(vec_loaded, 16)
            with act.Fori(0, E1A) as c:
                act.wait_ge(slab_done, done(c * SLOTS + 1))
                act.wait_ge(bank_free[1], c + 1)
                nc.scalar.activation(sig, bank[0][:, :], ACT.Sigmoid).then_inc(bank_free[0], 1)
                split_ahead(c, 1)
                act.wait_ge(bank_free[1], c + 2)
                nc.scalar.activation(tile(c + CB), glu[:, PAD - CONV_B + 1:PAD - CONV_B + 1 + T],
                                     ACT.Identity, bias=col("bias_b", c),
                                     scale=tap("conv_b", c, CONV_B, 0)).then_inc(seeded_b, 1)
                split_ahead(c, 2)
                act.wait_ge(slab_done, done(c * SLOTS + 3))
                act.wait_ge(bank_free[3], c + 1)
                nc.scalar.activation(a_c, bank[2][:, :], ACT.Copy).then_inc(bank_free[2], 1)
                split_ahead(c, 3)
                act.wait_ge(bank_free[3], c + 2)
                nc.scalar.activation(tile(c), prod[:, PAD - CONV_A + 1:PAD - CONV_A + 1 + T],
                                     ACT.Identity, bias=0.0,
                                     scale=tap("conv_a", c, CONV_A, 0)).then_inc(seeded_a, 1)
                split_ahead(c + 1, 0)

            def gate(q, step, n, buf):
                act.wait_ge(slab_done, done(step * SLOTS + (q + 1)))
                act.wait_ge(gated, n + 1)
                nc.scalar.activation(sz[buf], bank[q][:, :], ACT.Silu)\
                    .then_inc(bank_free[q], 1)

            def e1b(i, first=0):
                for q in range(first, 2):
                    split_ahead(i + E1A, q)
                gate(1, i + E1A, i * 2, 0)
                split_ahead(i + E1A, 2)
                split_ahead(i + E1A, 3)
                gate(3, i + E1A, i * 2 + 1, 1)

            e1b(0, 1)
            act.wait_ge(stat_ready, 1)
            nc.scalar.activation(mean, bank[4][:, :], ACT.Copy, scale=1.0 / W_A)\
                .then_inc(bank_free[4], 1)
            with act.Fori(1, E1B) as i:
                e1b(i)

            def u_rounded(first, last):
                for k in range(first, last):
                    act.wait_ge(gated, 2 + k + 1)
                    nc.scalar.activation(h_hi[:, k, :], rows[:, k, :], ACT.Copy)\
                        .then_inc(u_hi_ready, 1)

            def e1c(i, last=False):
                for q in range(SLOTS):
                    split_ahead(i + (E1A + E1B), q)
                    c = i * 4 + q
                    act.wait_ge(ln_scaled, c + 1)
                    nc.scalar.activation(tile(c + CB), tile(c + CB), ACT.Silu,
                                         bias=col("ln_b", c), scale=col("ln_g", c))\
                        .then_inc(ln_silu, 1)
                    if last and q == SLOTS - 1:
                        act.wait_ge(h_used, 1)
                        u_rounded(0, QUARTER)
                    gate(q, i + (E1A + E1B), i * 4 + (CB + q), q % 2)

            with act.Fori(0, E1C - 1) as i:
                e1c(i)
            e1c(E1C - 1, last=True)
            u_rounded(QUARTER, KT)

            def y_squares(t, step, first, layer, sets, nb):
                if t < TT - 1:
                    act.wait_ge(acc_ready, first * (TT - 1) + (layer * NBLK * (TT - 1) + t + 1))
                else:
                    act.wait_ge(slab_done, done(step * SLOTS + SLOTS))
                nc.scalar.activation(junk_y[t], bank[t][:, :], ACT.Square,
                                     accum_out=sumsq[:, sets[t], bass.ds(nb, 1)])\
                    .then_inc(y_squared, 1)

            def blocks(at, layer, sets):
                with act.Fori(0, NBLK - 1) as nb:
                    for q in range(SLOTS):
                        split_ahead(nb + at, q)
                    for t in range(TT):
                        y_squares(t, nb + at, nb, layer, sets, nb)
                split_ahead(at + NBLK - 1, 0)

            mid_sets = [MID + 2 * t for t in range(TT)]
            blocks(AT_E2, 0, mid_sets)
            end = AT_E2 + NBLK - 1

            def mid_norm(t, between=lambda: None):
                y_squares(t, end, NBLK - 1, 0, mid_sets, NBLK - 1)
                between()
                squares(tok[:, t, :], MID + 2 * t + 1,
                        lambda j: act.wait_ge(x_mid_ready, 4 * t + j + 1))
                act.dma_start(x_mid[t * P:(t + 1) * P, :], tok[:, t, :]).then_inc(mid_stored, 16)

            def mid_rounded(t):
                h_rounded(TT + t, t)
                if t + 2 < TT:
                    act.dma_start(resid[t % 2], x[(t + 2) * P:(t + 3) * P, :])\
                        .then_inc(resid_loaded[t % 2], 16)

            mid_norm(0)
            mid_norm(1)
            mid_rounded(0)
            mid_norm(2)
            mid_rounded(1)
            split_ahead(end, 1)

            def under_last_norm():
                mid_rounded(2)
                split_ahead(end, 2)
                split_ahead(end, 3)

            mid_norm(3, under_last_norm)
            split_ahead(end + 1, 0)
            mid_rounded(3)

            def values(g, first=0):
                for q in range(SLOTS):
                    if q >= first:
                        split_ahead(g + AT_O1, q)
                    act.wait_ge(slab_done, done(g * SLOTS + (AT_O1 * SLOTS + q + 1)))
                    act.wait_ge(v_used, g * 4 + (q + 1))
                    nc.scalar.activation(v_row[:, PAD:], bank[q][:, :], ACT.Copy)\
                        .then_inc(bank_free[q], 1)

            values(0, 1)
            with act.Fori(1, O1V) as g:
                values(g)

            def pooled_rounded(g):
                for k in range(4 * g, 4 * g + 4):
                    nc.scalar.activation(h_hi[:, k, :], rows[:, k, :], ACT.Copy)\
                        .then_inc(pool_hi_ready, 1)

            def gates(g, last=False):
                for q in range(SLOTS):
                    split_ahead(g + (AT_O1 + O1V), q)
                    if last and q == SLOTS - 1:
                        act.wait_ge(v_used, KT + 1)
                        act.wait_ge(h_used, 2)
                        pooled_rounded(0)
                    act.wait_ge(slab_done, done(g * SLOTS + ((AT_O1 + O1V) * SLOTS + q + 1)))
                    z = silu_z[:, bass.ds(g * 4 + q, 1), :].rearrange("p a t -> p (a t)")
                    nc.scalar.activation(z, bank[q][:, :], ACT.Silu).then_inc(bank_free[q], 1)

            with act.Fori(0, O1Z - 1) as g:
                gates(g)
            gates(O1Z - 1, last=True)

            def mapped_rounded(g):
                for m in range(4):
                    j = 4 * g + m
                    b = 4 + m if g % 2 else m
                    used = uses4(b, "map", g // 2) if g % 2 else AT_O1C + g // 2
                    act.wait_ge(bank_free[b], used + 2)
                    nc.scalar.activation(h_hi[:, j, :], rows[:, j, :], ACT.Copy)\
                        .then_inc(u_hi_ready, 1)

            for g in range(NG):
                if g > 0:
                    pooled_rounded(g)
                split_ahead(AT_O1C, g)
                if g > 0:
                    mapped_rounded(g - 1)
            mapped_rounded(NG - 1)

            post_sets = [POST1 + t for t in range(TT)]
            blocks(AT_O2, 1, post_sets)
            for t in range(TT):
                y_squares(t, AT_O2 + NBLK - 1, NBLK - 1, 1, post_sets, NBLK - 1)
                if t in (1, 2):
                    act.wait_ge(out_ready, 4 * t)
                    act.dma_start(resid[(t + 1) % 2], x_mid[(t + 1) * P:(t + 2) * P, :])\
                        .then_inc(resid_loaded[(t + 1) % 2], 16)

        @block.vector
        def _(dve):
            chain = [0, 0]

            def link(ins):
                chain[0] += 1
                ins.then_inc(dve_done, 1)
                dve.wait_ge(dve_done, chain[1] + chain[0])

            def split(slot, n):
                dve.wait_ge(hi_ready, n + 1)
                nc.vector.tensor_tensor(w_lo[:, slot, :], raw[:, slot % RAW, :],
                                        f32(w_hi[:, slot, :]), ALU.subtract)\
                    .then_inc(lo_ready, 1)

            def split_ahead(step, q):
                a = q + LOOKAHEAD
                split(a % SLOTS, step * SLOTS + a)

            def mean_square(n):
                link(nc.vector.reduce_sum(total[:, n:n + 1], sumsq[:, n, :], AX.X))
                nc.vector.tensor_scalar(meansq[:, n:n + 1], total[:, n:n + 1], 1.0 / D, EPS,
                                        ALU.mult, ALU.add).then_inc(mean_squared, 1)

            def scaled(dst, src, n, gain, by=lambda j: None):
                dve.wait_ge(rstd_ready, n + 1)
                for j in range(4):
                    by(j)
                    nc.vector.scalar_tensor_tensor(
                        out=part4(dst, j), in0=part4(src, j), scalar=rstd[:, n:n + 1],
                        in1=part4(gain, j), op0=ALU.mult, op1=ALU.mult).then_inc(normed, 1)

            def h_rest(n, t):
                for j in range(4):
                    dve.wait_ge(h_hi_ready, 4 * n + j + 1)
                    at = (slice(None), slice(4 * j, 4 * j + 4), slice(t * P, (t + 1) * P))
                    nc.vector.tensor_tensor(
                        h_lo[at], bank[4 + j][:, :].rearrange("p (k c) -> p k c", c=P),
                        f32(h_hi[at]), ALU.subtract).then_inc(bank_free[4 + j], 1)

            def x_normed(t):
                dve.wait_ge(squared, 4 * t + 4)
                mean_square(PRE0 + t)
                scaled(tok[:, t, :], tok[:, t, :], PRE0 + t, gain_pre,
                       lambda j: dve.wait_ge(gain_pre_loaded[j], 16))

            x_normed(0)
            x_normed(1)
            h_rest(0, 0)
            split(0, 0)
            h_rest(1, 1)
            split(1, 1)
            x_normed(2)
            split(2, 2)
            x_normed(3)
            h_rest(2, 2)
            split_ahead(0, 0)
            h_rest(3, 3)

            def convolve(c, taps, row, width, name, first, last):
                dst = tile(c + CB) if name == "conv_b" else tile(c)
                for j in range(first, last):
                    at = PAD - width + 1 + j
                    ins = nc.vector.scalar_tensor_tensor(
                        out=dst, in0=row[:, at:at + T], scalar=tap(name, c, width, j), in1=dst,
                        op0=ALU.mult, op1=ALU.add)
                    if taps is not None and j == width - 1:
                        ins.then_inc(taps, 1)
                    else:
                        link(ins)

            dve.wait_ge(vec_loaded, 16)
            dve.wait_ge(consts_set, 6)
            before, links = chain[0], CONV_B - 2 + CONV_A - 1
            with dve.Fori(0, E1A) as c:
                chain[1] = c * links
                split_ahead(c, 1)
                dve.wait_ge(slab_done, done(c * SLOTS + 2))
                dve.wait_ge(bank_free[0], c + 2)
                nc.vector.tensor_tensor(glu[:, PAD:], bank[1][:, :], sig, ALU.mult)\
                    .then_inc(bank_free[1], 1)
                dve.wait_ge(bank_free[1], c + 2)
                dve.wait_ge(seeded_b, c + 1)
                convolve(c, conv_done, glu, CONV_B, "conv_b", 1, 11)
                split_ahead(c, 2)
                convolve(c, conv_done, glu, CONV_B, "conv_b", 11, 21)
                split_ahead(c, 3)
                dve.wait_ge(slab_done, done(c * SLOTS + 4))
                dve.wait_ge(bank_free[2], c + 2)
                nc.vector.tensor_tensor(prod[:, PAD:], bank[3][:, :], a_c, ALU.mult)\
                    .then_inc(bank_free[3], 1)
                convolve(c, conv_done, glu, CONV_B, "conv_b", 21, CONV_B)
                dve.wait_ge(bank_free[3], c + 2)
                dve.wait_ge(seeded_a, c + 1)
                convolve(c, None, prod, CONV_A, "conv_a", 1, CONV_A)
                split_ahead(c + 1, 0)
            assert chain[0] == before + links
            chain[:] = before + links * E1A, 0

            def e1b(i, first=0, between=None):
                step = i + E1A
                for q in range(SLOTS):
                    c = i * 2 + q // 2
                    if q >= first:
                        split_ahead(step, q)
                    if q % 2 == 0:
                        dve.wait_ge(slab_done, done(step * SLOTS + (q + 1)))
                        nc.vector.tensor_tensor(tile(c), tile(c), bank[q][:, :], ALU.mult)\
                            .then_inc(bank_free[q], 1)
                    else:
                        dve.wait_ge(bank_free[q - 1], step + 2)
                        dve.wait_ge(bank_free[q], step + 2)
                        nc.vector.tensor_tensor(tile(c), tile(c), sz[q // 2], ALU.mult)\
                            .then_inc(gated, 1)
                        if between is not None and q == 1:
                            between()

            e1b(0, first=1)
            with dve.Fori(1, E1B - 1) as i:
                e1b(i)
            dve.wait_ge(stat_ready, 2)
            nc.vector.tensor_scalar(ln_var[:, :], bank[5][:, 0:TT], 1.0 / W_A, EPS,
                                    ALU.mult, ALU.add).then_inc(bank_free[5], 1)

            def make_diagonals():
                dve.wait_ge(ln_rstd_ready, 1)
                for t in range(TT):
                    nc.vector.tensor_scalar(diagonals[:, t, :], ident[:, :],
                                            ln_power[:, t:t + 1], None, ALU.mult)\
                        .then_inc(diagonals_ready, 1)

            e1b(E1B - 1, between=make_diagonals)

            dve.wait_ge(stat_ready, 3)
            nc.vector.tensor_copy(ln_rstd, bank[6][:, :]).then_inc(bank_free[6], 1)
            dve.wait_ge(bank_free[6], uses4(6, "stat") + 2)

            def u_rest(j, n):
                dve.wait_ge(u_hi_ready, n + 1)
                nc.vector.tensor_tensor(h_lo[:, j, :], rows[:, j, :], f32(h_hi[:, j, :]),
                                        ALU.subtract).then_inc(u_lo_ready, 1)

            def e1c(i, last=False):
                for q in range(SLOTS):
                    c = i * 4 + q
                    nc.vector.tensor_tensor(tile(c + CB), tile(c + CB), ln_rstd, ALU.mult)\
                        .then_inc(ln_scaled, 1)
                    split_ahead(i + (E1A + E1B), q)
                    if last and q == SLOTS - 1:
                        for k in range(QUARTER):
                            u_rest(k, k)
                    dve.wait_ge(ln_silu, c + 1)
                    dve.wait_ge(bank_free[q], i + (E1A + E1B + 2))
                    nc.vector.tensor_tensor(tile(c + CB), tile(c + CB), sz[q % 2], ALU.mult)\
                        .then_inc(gated, 1)

            with dve.Fori(0, E1C - 1) as i:
                e1c(i)
            e1c(E1C - 1, last=True)
            for k in range(QUARTER, KT):
                u_rest(k, k)

            def y_gained(t, nb, count):
                dve.wait_ge(y_squared, count + (t + 1))
                nc.vector.tensor_tensor(tok[:, t, bass.ds(nb * T, T)], bank[t][:, :],
                                        gain_post[:, bass.ds(nb * T, T)], ALU.mult)\
                    .then_inc(bank_free[t], 1)

            def blocks(at, layer):
                with dve.Fori(0, NBLK - 1) as nb:
                    for q in range(SLOTS):
                        split_ahead(nb + at, q)
                    for t in range(TT):
                        y_gained(t, nb, nb * TT + layer * NBLK * TT)
                split_ahead(at + NBLK - 1, 0)

            def added(t, n, layer, used, ready, between=lambda: None):
                y_gained(t, NBLK - 1, (layer * NBLK + NBLK - 1) * TT)
                mean_square(n)
                between()
                dve.wait_ge(bank_free[t], used + 2)
                dve.wait_ge(rstd_ready, n + 1)
                dve.wait_ge(resid_loaded[t % 2], 16 * (2 * layer + t // 2 + 1))
                for j in range(4):
                    nc.vector.scalar_tensor_tensor(
                        out=part4(tok[:, t, :], j), in0=part4(tok[:, t, :], j),
                        scalar=rstd[:, n:n + 1], in1=part4(resid[t % 2], j),
                        op0=ALU.mult, op1=ALU.add).then_inc(ready, 1)

            dve.wait_ge(gain_end_loaded, 32)
            blocks(AT_E2, 0)
            end = AT_E2 + NBLK - 1

            def mid_norm(t, first=lambda: None, second=lambda: None):
                added(t, MID + 2 * t, 0, end, x_mid_ready, first)
                second()
                dve.wait_ge(squared, 4 * (TT + t) + 4)
                mean_square(MID + 2 * t + 1)
                scaled(resid[t % 2], tok[:, t, :], MID + 2 * t + 1, gain_next)

            mid_norm(0)
            mid_norm(1)
            h_rest(TT + 0, 0)
            mid_norm(2)
            h_rest(TT + 1, 1)
            split_ahead(end, 1)

            def under_last_norm():
                h_rest(TT + 2, 2)
                split_ahead(end, 2)

            mid_norm(3, under_last_norm, lambda: split_ahead(end, 3))
            split_ahead(end + 1, 0)
            h_rest(TT + 3, 3)

            dve.wait_ge(mid_stored, 16 * TT)
            for g, window in enumerate(WINDOWS):
                for q in range(SLOTS):
                    j = 4 * g + q
                    if j > 0:
                        split_ahead(AT_O1 + g, q)
                    dve.wait_ge(bank_free[q], AT_O1 + g + 2)
                    src, step = v_row, 1
                    while step < window:
                        dst = sum_a if src is not sum_a else sum_b
                        link(nc.vector.tensor_tensor(
                            dst[:, PAD:], src[:, PAD:], src[:, PAD - step:PAD - step + T],
                            ALU.add))
                        src, step = dst, 2 * step
                    start = src[:, PAD:PAD + window]
                    rest = slice(PAD + window, PAD + T)
                    nc.vector.scalar_tensor_tensor(
                        out=rows[:, j, window:], in0=src[:, rest], scalar=1.0 / window,
                        in1=v_row[:, rest], op0=ALU.mult, op1=ALU.subtract)
                    link(nc.vector.tensor_tensor(start, start, inv_count[:, 0:window],
                                                       ALU.mult))
                    nc.vector.tensor_tensor(rows[:, j, 0:window], start,
                                            v_row[:, PAD:PAD + window], ALU.subtract)\
                        .then_inc(v_used, 1)
            with dve.Fori(0, O1Z) as g:
                for q in range(SLOTS):
                    split_ahead(g + (AT_O1 + O1V), q)
                    dve.wait_ge(bank_free[q], g + (AT_O1 + O1V + 2))
                    z = silu_z[:, bass.ds(g * 4 + q, 1), :].rearrange("p a t -> p (a t)")
                    nc.vector.tensor_scalar(z, z, col("c_scale", g * 4 + q), None, ALU.mult)\
                        .then_inc(z_scaled, 1)

            def group(g):
                dve.wait_ge(slab_done, done(AT_O1C * SLOTS + g + 1))
                for m in range(4):
                    j, b = 4 * g + m, (4 + m if g % 2 else m)
                    nc.vector.scalar_tensor_tensor(
                        out=rows[:, j, :], in0=bank[b][:, :], scalar=col("c_b", j),
                        in1=silu_z[:, j, :], op0=ALU.add, op1=ALU.mult)\
                        .then_inc(bank_free[b], 1)
                for j in range(4 * g, 4 * g + 4):
                    u_rest(j, KT + j)

            dve.wait_ge(z_scaled, KT)
            for g in range(NG):
                split_ahead(AT_O1C, g)
                if g > 0:
                    group(g - 1)
            group(NG - 1)

            dve.wait_ge(gain_end_loaded, 48)
            blocks(AT_O2, 1)
            for t in range(TT):
                added(t, POST1 + t, 1, AT_O2 + NBLK, out_ready)


def kernel(**inputs):
    import concourse.bacc as bacc
    from concourse.bass_utils import run_bass_kernel_spmd

    conv_b = np.asarray(inputs["e_b_conv"]).reshape(CONV_B, CB, P).transpose(2, 1, 0)
    conv_a = np.asarray(inputs["e_a_conv"]).reshape(CONV_A, CB, P).transpose(2, 1, 0)
    packed = [conv_b.reshape(P, -1), conv_a.reshape(P, -1)]
    for name, tiles in (("e_b_conv_bias", CB), ("e_b_ln_g", CB), ("e_b_ln_b", CB),
                        ("o_c_b", KT), ("o_c_scale", KT)):
        packed.append(np.asarray(inputs[name]).reshape(tiles, P).T)
    arrays = {
        "x": np.asarray(inputs["x"]).reshape(T, D),
        "vec": np.concatenate(packed, axis=1),
        "e_pre": np.asarray(inputs["e_norm_pre"]),
        "e_post": np.asarray(inputs["e_norm_post"]),
        "e_in": np.asarray(inputs["e_w_in"])[0],
        "e_out": np.asarray(inputs["e_w_out"])[0],
        "o_pre": np.asarray(inputs["o_norm_pre"]),
        "o_post": np.asarray(inputs["o_norm_post"]),
        "o_in": np.asarray(inputs["o_w_in"])[0],
        "o_cw": np.asarray(inputs["o_c_w"])[0],
        "o_out": np.asarray(inputs["o_w_out"])[0],
    }
    arrays = {name: np.ascontiguousarray(a) for name, a in arrays.items()}
    nc = bacc.Bacc("TRN2", target_bir_lowering=False, num_devices=1,
                   dynamic_dma_scratch_size=1024)
    aps = [nc.dram_tensor(name, a.shape, F32, kind="ExternalInput").ap()
           for name, a in arrays.items()]
    result = nc.dram_tensor("out", (T, D), F32, kind="ExternalOutput").ap()
    build(nc, *aps, result)
    got = run_bass_kernel_spmd(nc, [arrays], core_ids=[0]).results[0]["out"]
    return got.reshape(inputs["x"].shape)
```

```python
from contextlib import ExitStack

import numpy as np

import concourse.bass as bass
from concourse import mybir

F32 = mybir.dt.float32
F32R = mybir.dt.float32r
BF16 = mybir.dt.bfloat16
ALU = mybir.AluOpType
ACT = mybir.ActivationFunctionType
AX = mybir.AxisListType

P = 128
D = 2048
T = 512
TT = T // P
KT = D // P
QUARTER = KT // 4
HALF = T // 2
SUM_BANKS = (4, 7)
W_A = D // 2
CB = W_A // P
CONV_A, CONV_B = 3, 31
WINDOWS = (2, 4, 8, 16)
NG = len(WINDOWS)
EPS = 1e-6

SLAB = 2048
SLOTS = 4
RAW = 2
LOOKAHEAD = SLOTS - 1
NBLK = D // T
PAD = 32

E1A = CB
E1B = CB // 2
E1C = CB // 4
E1 = E1A + E1B + E1C
E2 = NBLK
O1V = O1Z = KT // 4
O1C = 1
AT_E2 = E1
AT_O1 = AT_E2 + E2
AT_O1C = AT_O1 + O1V + O1Z
AT_O2 = AT_O1C + O1C

A_X, A_B, A_C, A_Z, B_VAL, B_GATE, B_Z = (n * W_A for n in range(7))

MID = 0
POST1 = 2 * TT
SETS = 3 * TT

VECTORS = (("conv_b", CB * CONV_B), ("conv_a", CB * CONV_A), ("bias_b", CB), ("ln_g", CB),
           ("ln_b", CB), ("c_b", KT), ("c_scale", KT), ("pre", KT))
AT_VEC = {name: sum(n for _, n in VECTORS[:i]) for i, (name, _) in enumerate(VECTORS)}
NVEC = sum(n for _, n in VECTORS)


def build(nc, x, x_t, vec, e_post, e_in, e_out, o_pre, o_post, o_in, o_cw, o_out, out):
    ctx = ExitStack()
    with ctx:
        def sb(name, shape, dt=F32):
            return ctx.enter_context(nc.sbuf_tensor(name, shape, dt))

        def sem(name):
            return ctx.enter_context(nc.semaphore(name))

        h_hi = sb("h_hi", [P, KT, T], F32R)
        h_lo = sb("h_lo", [P, KT, T], F32R)
        rows = sb("rows", [P, KT, T])
        tok = rows[:, :, :].rearrange("p (t a) c -> p t (a c)", t=TT)
        raw = sb("raw", [P, RAW, SLAB])
        w_hi = sb("w_hi", [P, SLOTS, SLAB], F32R)
        w_lo = sb("w_lo", [P, SLOTS, SLAB], F32R)
        scratch = sb("scratch", [P, KT * T])
        shifted = sb("shifted", [P, 3, PAD + T])
        vecs = sb("vecs", [P, NVEC])
        ident = sb("ident", [P, P])
        ones = sb("ones", [P, P])
        inv_count = sb("inv_count", [P, WINDOWS[-1]])
        minus_half = sb("minus_half", [P, 1])
        junk = sb("junk", [P, 2, T], BF16)
        sumsq = sb("sumsq", [P, SETS, NBLK])
        total = sb("total", [P, SETS])
        meansq = sb("meansq", [P, SETS])
        rstd = sb("rstd", [P, SETS])
        token_var = sb("token_var", [P, TT])
        token_power = sb("token_power", [P, TT])
        diagonals = sb("diagonals", [P, TT, P])

        sig, a_c, csum, mean, vsum, ln_rstd, sq, sz0, sz1 = (
            scratch[:, n * T:(n + 1) * T] for n in range(9))
        x_partial = scratch[:, 0:4 * HALF].rearrange("p (k t) -> p k t", k=4)
        x_sq = scratch[:, KT * T // 2:].rearrange("p (j k t) -> p j k t", j=4, k=QUARTER)
        sz = (sz0, sz1)
        gain_post, gain_next, resid0, resid1 = (scratch[:, n * D:(n + 1) * D] for n in range(4))
        resid = (resid0, resid1)
        silu_z = scratch[:, :].rearrange("p (j t) -> p j t", j=KT)

        glu, prod = shifted[:, 0, :], shifted[:, 1, :]
        v_row, sum_a, sum_b = (shifted[:, n, :] for n in range(3))
        junk_y = [shifted[:, t // 2, PAD:].bitcast(BF16)[:, t % 2 * T:(t % 2 + 1) * T]
                  for t in range(TT)]

        bank = [ctx.enter_context(nc.psum_tensor(f"bank{b}", [P, T], F32)) for b in range(8)]

        x_mid = nc.dram_tensor("x_mid", [T, D], F32, kind="Internal").ap()

        x_loaded = [[sem(f"x_loaded{h}{j}") for j in range(4)] for h in range(2)]
        first_loaded = [[sem(f"first_loaded{n}{j}") for j in range(4)] for n in range(RAW)]
        first_hi = sem("first_hi")
        first_lo = sem("first_lo")
        first_lo_pool = sem("first_lo_pool")
        x_squared = sem("x_squared")
        x_reduced = sem("x_reduced")
        x_added = sem("x_added")
        x_summed = sem("x_summed")
        x_power_ready = sem("x_power_ready")
        x_spread = sem("x_spread")
        x_normed = sem("x_normed")
        x_hi_ready = sem("x_hi_ready")
        x_lo_ready = sem("x_lo_ready")
        vec_loaded = sem("vec_loaded")
        gain_end_loaded = sem("gain_end_loaded")
        resid_loaded = [sem(f"resid_loaded{s}") for s in range(2)]
        mid_stored = sem("mid_stored")
        out_stored = sem("out_stored")
        consts_set = sem("consts_set")
        pool_done = sem("pool_done")
        raw_loaded = [sem(f"raw_loaded{s}") for s in range(RAW)]
        hi_ready = sem("hi_ready")
        lo_ready = sem("lo_ready")
        slab_done = sem("slab_done")
        h_used = sem("h_used")
        acc_ready = sem("acc_ready")
        bank_free = [sem(f"bank_free{b}") for b in range(8)]
        transposed = sem("transposed")
        stat_ready = sem("stat_ready")
        squared = sem("squared")
        mean_squared = sem("mean_squared")
        rstd_ready = sem("rstd_ready")
        normed = sem("normed")
        h_hi_ready = sem("h_hi_ready")
        dve_done = sem("dve_done")
        seeded_b = sem("seeded_b")
        seeded_a = sem("seeded_a")
        conv_done = sem("conv_done")
        csum_ready = sem("csum_ready")
        vsum_ready = sem("vsum_ready")
        ln_rstd_ready = sem("ln_rstd_ready")
        diagonals_ready = sem("diagonals_ready")
        ln_scaled = sem("ln_scaled")
        ln_silu = sem("ln_silu")
        gated = sem("gated")
        u_hi_ready = sem("u_hi_ready")
        u_lo_ready = sem("u_lo_ready")
        y_squared = sem("y_squared")
        x_mid_ready = sem("x_mid_ready")
        z_scaled = sem("z_scaled")
        v_used = sem("v_used")
        pool_hi_ready = sem("pool_hi_ready")
        pool_lo_ready = sem("pool_lo_ready")
        out_ready = sem("out_ready")

        def f32(ap):
            return ap.bitcast(F32)

        def col(name, n, step=1):
            return vecs[:, bass.ds(n * step + AT_VEC[name], 1)]

        def tap(name, c, taps, j):
            return vecs[:, bass.ds(c * taps + (AT_VEC[name] + j), 1)]

        def tile(n):
            if isinstance(n, int):
                return rows[:, n, :]
            return rows[:, bass.ds(n, 1), :].rearrange("p a t -> p (a t)")

        def done(n):
            return n + SLOTS

        def uses4(b, part, n=0):
            x_norm, layer_norm = {4: (2, 1), 5: (1, 1), 6: (1, 1), 7: (2, 0)}[b]
            mid = x_norm + layer_norm
            return {"x": 0, "stat": x_norm, "mid": mid, "map": mid + TT}[part] + n

        def x_half(h, k, count):
            return slice(None), slice(k, k + count), slice(h * HALF, (h + 1) * HALF)

        def part4(ap, j):
            return ap[:, j * T:(j + 1) * T]

        block = ctx.enter_context(nc.Block())

        @block.sync
        def _(sp):
            def load_x(h):
                for j in range(4):
                    sp.dma_start(rows[x_half(h, j * QUARTER, QUARTER)],
                                 x_t.rearrange("(k p) t -> p k t", p=P)
                                 [x_half(h, j * QUARTER, QUARTER)])\
                        .then_inc(x_loaded[h][j], 16)

            load_x(0)

            def load(slot, src, n):
                sp.wait_ge(lo_ready, n - (RAW - 1))
                dst = raw[:, slot % RAW, :].rearrange("p (k c) -> p k c", c=src.shape[-1])
                sp.dma_start(dst, src).then_inc(raw_loaded[slot % RAW], 16)

            def columns(w, first):
                return w.rearrange("(k p) n -> p k n", p=P)[:, :, bass.ds(first, P)]

            def block_part(w, nb, q):
                v = w.rearrange("(k p) n -> p k n", p=P)
                return v[:, q * KT // 4:(q + 1) * KT // 4, bass.ds(nb * T, T)]

            E1A_ORDER = (B_GATE, B_VAL, A_C, A_X)
            for j in range(4):
                for n in range(RAW):
                    part = slice(j * QUARTER, (j + 1) * QUARTER)
                    sp.dma_start(raw[:, n, j * T:(j + 1) * T].rearrange("p (k c) -> p k c", c=P),
                                 columns(e_in, E1A_ORDER[n])[:, part, :])\
                        .then_inc(first_loaded[n][j], 16)
                if j == 1:
                    sp.dma_start(vecs[:, :], vec).then_inc(vec_loaded, 16)
            load_x(1)
            sp.wait_ge(first_lo, 2 * RAW)
            for q in range(RAW, SLOTS):
                load(q, columns(e_in, E1A_ORDER[q]), q)
            with sp.Fori(0, E1A - 1) as i:
                for q, kind in enumerate(E1A_ORDER):
                    load(q, columns(e_in, i * P + (P + kind)), i * SLOTS + (SLOTS + q))
            with sp.Fori(0, E1B) as i:
                for q, kind in enumerate((A_B, A_Z, A_B + P, A_Z + P)):
                    load(q, columns(e_in, i * (2 * P) + kind), i * SLOTS + (E1A * SLOTS + q))
            with sp.Fori(0, E1C) as i:
                for q in range(SLOTS):
                    load(q, columns(e_in, i * (4 * P) + (B_Z + q * P)),
                         i * SLOTS + ((E1A + E1B) * SLOTS + q))

            def token_major_loads(w, step, gains, rows_in, u_tiles):
                for q in range(SLOTS):
                    load(q, block_part(w, 0, q), step * SLOTS + q)
                sp.wait_ge(u_lo_ready, u_tiles)
                for dst, src in gains:
                    sp.dma_start(dst, src.to_broadcast([P, D])).then_inc(gain_end_loaded, 16)
                for t in range(2):
                    sp.dma_start(resid[t], rows_in[t * P:(t + 1) * P, :])\
                        .then_inc(resid_loaded[t], 16)
                with sp.Fori(1, NBLK) as nb:
                    for q in range(SLOTS):
                        load(q, block_part(w, nb, q), nb * SLOTS + (step * SLOTS + q))

            token_major_loads(e_out, AT_E2, ((gain_post, e_post), (gain_next, o_pre)), x, KT)
            with sp.Fori(0, O1V + O1Z) as g:
                for q in range(SLOTS):
                    load(q, columns(o_in, g * (4 * P) + q * P), g * SLOTS + (AT_O1 * SLOTS + q))
            for g in range(NG):
                load(g, o_cw[g].rearrange("(k p) n -> p k n", p=P), AT_O1C * SLOTS + g)
            token_major_loads(o_out, AT_O2, ((gain_post, o_post),), x_mid, 2 * KT)
            for t in range(TT - 1):
                sp.wait_ge(out_ready, 4 * t + 4)
                sp.dma_start(out[t * P:(t + 1) * P, :], tok[:, t, :]).then_inc(out_stored, 16)
            for j in range(4):
                sp.wait_ge(out_ready, 4 * (TT - 1) + j + 1)
                sp.dma_start(out[(TT - 1) * P:, j * T:(j + 1) * T],
                             part4(tok[:, TT - 1, :], j)).then_inc(out_stored, 16)
            sp.wait_ge(out_stored, 16 * (TT - 1 + 4))

        @block.gpsimd
        def _(pool):
            for b in range(8):
                pool.sem_inc(bank_free[b], 1)
            pool.sem_inc(gated, 2)
            pool.sem_inc(v_used, 1)
            nc.gpsimd.memset(ident[:, :], 0.0).then_inc(pool_done, 1)
            pool.wait_ge(pool_done, 1)
            nc.gpsimd.affine_select(out=ident[:, :], in_=ident[:, :], compare_op=ALU.not_equal,
                                    fill=1.0, base=0, pattern=[[-1, P]],
                                    channel_multiplier=1).then_inc(consts_set, 1)
            nc.gpsimd.memset(minus_half[:, :], -0.5).then_inc(consts_set, 1)
            nc.gpsimd.memset(ones[:, :], 1.0).then_inc(consts_set, 1)
            nc.gpsimd.memset(shifted[:, :, 0:PAD], 0.0).then_inc(consts_set, 1)
            nc.gpsimd.memset(csum, 0.0).then_inc(consts_set, 1)
            nc.gpsimd.memset(vsum, 0.0).then_inc(consts_set, 1)
            for n in range(WINDOWS[-1]):
                nc.gpsimd.memset(inv_count[:, n:n + 1], 1.0 / (n + 1)).then_inc(consts_set, 1)
            pool.wait_ge(consts_set, 6)

            def x_power(h):
                for b in SUM_BANKS:
                    pool.wait_ge(bank_free[b], uses4(b, "x", h) + 2)
                at = (slice(None), slice(h * TT // 2, (h + 1) * TT // 2))
                nc.gpsimd.tensor_tensor(token_power[at], token_var[at],
                                        minus_half[:, 0:1].to_broadcast([P, TT // 2]),
                                        ALU.pow).then_inc(x_power_ready, 1)

            x_power(0)

            def quarter_rest(slot, j):
                part = slice(j * T, (j + 1) * T)
                nc.gpsimd.tensor_tensor(w_lo[:, slot, part], raw[:, slot % RAW, part],
                                        f32(w_hi[:, slot, part]), ALU.subtract)\
                    .then_inc(lo_ready if j == 3 else first_lo_pool, 1)

            for j in range(2, 4):
                for n in range(RAW):
                    pool.wait_ge(first_hi, RAW * j + n + 1)
                    quarter_rest(n, j)
            for j in range(1, 4):
                pool.wait_ge(x_squared, 4 + j + 1)
                nc.gpsimd.tensor_tensor(x_sq[:, 0, :, :], x_sq[:, 0, :, :], x_sq[:, j, :, :],
                                        ALU.add).then_inc(x_added, 1)
                pool.wait_ge(x_added, j)
            pool.wait_ge(hi_ready, RAW + 1)
            for j in range(4):
                quarter_rest(RAW, j)
            x_power(1)

            def powers(first, count):
                for n in range(first, first + count):
                    pool.wait_ge(mean_squared, n + 1)
                    nc.gpsimd.tensor_tensor(rstd[:, n:n + 1], meansq[:, n:n + 1],
                                            minus_half[:, :], ALU.pow).then_inc(rstd_ready, 1)

            for c in range(CB):
                pool.wait_ge(conv_done, c + 1)
                nc.gpsimd.tensor_tensor(csum, csum, tile(c + CB), ALU.add)\
                    .then_inc(csum_ready, 1)
                pool.wait_ge(csum_ready, c + 1)

            pool.wait_ge(bank_free[4], uses4(4, "stat") + 2)
            for c in range(CB):
                nc.gpsimd.tensor_tensor(tile(c + CB), tile(c + CB), mean, ALU.subtract)\
                    .then_inc(pool_done, 1)
                pool.wait_ge(pool_done, c * 2 + 2)
                nc.gpsimd.tensor_tensor(sq, tile(c + CB), tile(c + CB), ALU.mult)\
                    .then_inc(pool_done, 1)
                pool.wait_ge(pool_done, c * 2 + 3)
                nc.gpsimd.tensor_tensor(vsum, vsum, sq, ALU.add).then_inc(vsum_ready, 1)
                pool.wait_ge(vsum_ready, c + 1)

            pool.wait_ge(bank_free[5], uses4(5, "stat") + 2)
            nc.gpsimd.tensor_tensor(token_power[:, :], token_var[:, :],
                                    minus_half[:, 0:1].to_broadcast([P, TT]),
                                    ALU.pow).then_inc(ln_rstd_ready, 1)

            powers(MID, 2 * TT)

            for k in range(KT):
                pool.wait_ge(pool_hi_ready, k + 1)
                nc.gpsimd.tensor_tensor(h_lo[:, k, :], rows[:, k, :], f32(h_hi[:, k, :]),
                                        ALU.subtract).then_inc(pool_lo_ready, 1)

            powers(POST1, TT)

        @block.tensor
        def _(pe):
            pe.sem_inc(slab_done, SLOTS)
            pe.wait_ge(consts_set, 3)

            def product(dst, w, m, first, last):
                nc.tensor.matmul(dst, w[0], m[0], start=first, stop=False)
                nc.tensor.matmul(dst, w[0], m[1], start=False, stop=False)
                return nc.tensor.matmul(dst, w[1], m[0], start=False, stop=last)

            def weights(slot, k, width):
                return (w_hi[:, slot, k * width:(k + 1) * width],
                        w_lo[:, slot, k * width:(k + 1) * width])

            def operand(k, first=0, width=T):
                return h_hi[:, k, first:first + width], h_lo[:, k, first:first + width]

            def feature_major(step, last_of_h=False):
                for q in range(SLOTS):
                    pe.wait_ge(lo_ready, step * SLOTS + (q + 1))
                    pe.wait_ge(bank_free[q], step + 1)
                    for k in range(KT):
                        last = product(bank[q][:, :], weights(q, k, P), operand(k),
                                       k == 0, k == KT - 1)
                        if last_of_h and q == SLOTS - 1 and k == QUARTER - 1:
                            last.then_inc(h_used, 1)
                    last.then_inc(slab_done, 1)

            def transposes(t, row):
                for j in range(4):
                    pe.wait_ge(normed, 4 * t + j + 1)
                    pe.wait_ge(bank_free[4 + j], uses4(4 + j, "mid", t) + 1)
                    for i in range(4):
                        k = 4 * j + i
                        last = nc.tensor.transpose(bank[4 + j][:, i * P:(i + 1) * P],
                                                   row[:, k * P:(k + 1) * P], ident[:, :])
                    last.then_inc(transposed, 1)

            def half_product(q, h, k):
                at = slice(h * HALF, (h + 1) * HALF)
                return product(bank[q][:, at], weights(q, k, P), operand(k, h * HALF, HALF),
                               k == 0, k == KT - 1)

            def half_slab(q, h, ready):
                for k in range(KT):
                    ready(k)
                    last = half_product(q, h, k)
                if h == 1:
                    last.then_inc(slab_done, 1)

            def slab_wait(step, q):
                pe.wait_ge(lo_ready, step * SLOTS + q + 1)
                pe.wait_ge(bank_free[q], step + 1)

            def x_sums(h, squares, ready):
                for b in SUM_BANKS:
                    pe.wait_ge(bank_free[b], uses4(b, "x", h) + 1)
                for j in range(4):
                    ready(j)
                    for t, b in enumerate(SUM_BANKS):
                        last = nc.tensor.matmul(bank[b][:, 0:1],
                                                squares[:, j, t * P:(t + 1) * P],
                                                ones[:, 0:1], start=j == 0, stop=j == 3)
                last.then_inc(x_summed, 1)

            def x_spread_out(h):
                pe.wait_ge(diagonals_ready, (h + 1) * TT // 2)
                pe.wait_ge(bank_free[5 + h], uses4(5 + h, "x") + 1)
                nc.tensor.matmul(bank[5 + h][:, 0:HALF], ones[:, :],
                                 diagonals[:, h * TT // 2:(h + 1) * TT // 2, :],
                                 start=True, stop=True).then_inc(x_spread, 1)

            def x_ready(h, k):
                if k % 2 == 0:
                    pe.wait_ge(x_lo_ready, h * KT // 2 + k // 2 + 1)

            def keep_warm(count):
                for _ in range(count):
                    nc.tensor.matmul(bank[0][:, 0:P], ones[:, :], ident[:, :],
                                     start=True, stop=True)

            for q in range(RAW):
                pe.wait_ge(bank_free[q], 1)
            x_sums(0, x_partial, lambda j: pe.wait_ge(x_reduced, j + 1))
            keep_warm(4)
            x_spread_out(0)
            keep_warm(5)
            for k in range(KT):
                for q in range(RAW):
                    if k % QUARTER == 0:
                        at = RAW * (k // QUARTER) + q + 1
                        if k < 2 * QUARTER:
                            pe.wait_ge(first_lo, at)
                        elif k < 3 * QUARTER:
                            pe.wait_ge(first_lo_pool, at - 2 * RAW)
                        else:
                            pe.wait_ge(lo_ready, q + 1)
                    x_ready(0, k)
                    half_product(q, 0, k)

            def slab_2_ready(k):
                if k % QUARTER == 0 and k < 3 * QUARTER:
                    pe.wait_ge(first_lo_pool, RAW + k // QUARTER + 1)
                elif k % QUARTER == 0:
                    pe.wait_ge(lo_ready, RAW + 1)
                if k == 2 * QUARTER:
                    x_sums(1, x_sq[:, 0, :, :], lambda j: pe.wait_ge(x_added, 3))

            pe.wait_ge(bank_free[RAW], 1)
            half_slab(RAW, 0, slab_2_ready)
            slab_wait(0, 3)
            half_slab(3, 0, lambda k: x_spread_out(1) if k == QUARTER else None)
            for k in range(KT):
                for q in range(RAW):
                    x_ready(1, k)
                    last = half_product(q, 1, k)
                    if k == KT - 1:
                        last.then_inc(slab_done, 1)
            for q in range(RAW, SLOTS):
                half_slab(q, 1, lambda k: None)
            with pe.Fori(1, E1A + 1) as i:
                feature_major(i)
            pe.wait_ge(csum_ready, CB)
            pe.wait_ge(bank_free[4], uses4(4, "stat") + 1)
            nc.tensor.matmul(bank[4][:, :], ones[:, :], csum, start=True, stop=True)\
                .then_inc(stat_ready, 1)
            with pe.Fori(E1A + 1, E1A + E1B - 1) as i:
                feature_major(i)
            pe.wait_ge(vsum_ready, CB)
            pe.wait_ge(bank_free[5], uses4(5, "stat") + 1)
            for t in range(TT):
                last = nc.tensor.matmul(bank[5][:, t:t + 1], vsum[:, t * P:(t + 1) * P],
                                        ones[:, 0:1], start=True, stop=True)
            last.then_inc(stat_ready, 1)
            feature_major(E1A + E1B - 1)
            pe.wait_ge(diagonals_ready, 2 * TT)
            pe.wait_ge(bank_free[6], uses4(6, "stat") + 1)
            nc.tensor.matmul(bank[6][:, :], ones[:, :], diagonals[:, :, :],
                             start=True, stop=True)\
                .then_inc(stat_ready, 1)
            with pe.Fori(E1A + E1B, E1 - 1) as i:
                feature_major(i)
            feature_major(E1 - 1, last_of_h=True)

            def token_major(step, extra, u_first):
                for q in range(SLOTS):
                    pe.wait_ge(lo_ready, step * SLOTS + (q + 1))
                    for kk in range(4):
                        k = 4 * q + kk
                        pe.wait_ge(u_lo_ready, u_first + k + 1)
                        for t in range(TT):
                            if k == 0:
                                pe.wait_ge(bank_free[t], step + (1 + extra))
                            last = product(bank[t][:, :], operand(k, t * P, P),
                                           weights(q, kk, T), k == 0, k == KT - 1)
                            if k == KT - 1 and t < TT - 1:
                                last.then_inc(acc_ready, 1)
                    last.then_inc(slab_done, 1)

            def token_major_last(step, extra, between):
                for t in range(TT):
                    pe.wait_ge(bank_free[t], step + 1 + extra)
                    for q in range(SLOTS):
                        if t == 0:
                            pe.wait_ge(lo_ready, step * SLOTS + q + 1)
                        for kk in range(4):
                            k = 4 * q + kk
                            last = product(bank[t][:, :], operand(k, t * P, P),
                                           weights(q, kk, T), k == 0, k == KT - 1)
                        if t == TT - 1:
                            last.then_inc(slab_done, 1)
                    if t < TT - 1:
                        last.then_inc(acc_ready, 1)
                    between(t)

            def mid_transposes(t):
                if t > 0:
                    transposes(t - 1, resid[(t - 1) % 2])

            def mid_split(h, k):
                if k % QUARTER == 0:
                    b = 4 + k // QUARTER
                    pe.wait_ge(bank_free[b], uses4(b, "mid", (h + 1) * TT // 2) + 1)

            with pe.Fori(0, NBLK - 1) as nb:
                token_major(nb + AT_E2, 0, 0)
            token_major_last(AT_E2 + NBLK - 1, 0, mid_transposes)
            for h in range(2):
                for q in range(SLOTS):
                    if h == 0:
                        slab_wait(AT_O1, q)
                    half_slab(q, h, lambda k: mid_split(h, k) if q == 0 else None)
                    if h == 0 and q == 2:
                        mid_transposes(TT)
            with pe.Fori(AT_O1 + 1, AT_O1C - 1) as i:
                feature_major(i)
            feature_major(AT_O1C - 1, last_of_h=True)
            for g in range(NG):
                half = 4 if g % 2 else 0
                pe.wait_ge(lo_ready, AT_O1C * SLOTS + g + 1)
                for k in range(4):
                    pe.wait_ge(pool_lo_ready, 4 * g + k + 1)
                    for m in range(4):
                        b = half + m
                        if k == 0:
                            used = uses4(b, "map", g // 2) if half else AT_O1C + g // 2
                            pe.wait_ge(bank_free[b], used + 1)
                        w = (w_hi[:, g, k * T + m * P:k * T + (m + 1) * P],
                             w_lo[:, g, k * T + m * P:k * T + (m + 1) * P])
                        last = product(bank[b][:, :], w, operand(4 * g + k), k == 0, k == 3)
                last.then_inc(slab_done, 1)
            with pe.Fori(0, NBLK - 1) as nb:
                token_major(nb + AT_O2, 1, KT)
            token_major_last(AT_O2 + NBLK - 1, 1, lambda t: None)

        @block.scalar
        def _(act):
            act.sem_inc(hi_ready, RAW)

            def split(slot, n, turn):
                act.wait_ge(raw_loaded[slot % RAW], turn * 16)
                act.wait_ge(slab_done, done(n - SLOTS) + 1)
                nc.scalar.activation(w_hi[:, slot, :], raw[:, slot % RAW, :], ACT.Copy)\
                    .then_inc(hi_ready, 1)

            def split_ahead(step, q):
                a = q + LOOKAHEAD
                split(a % SLOTS, step * SLOTS + a, step * (SLOTS // RAW) + a // RAW)

            def squares(src, n, t, by):
                for j in range(4):
                    by(j)
                    count = 4 * t + j
                    if count >= 2:
                        act.wait_ge(squared, count - 1)
                    nc.scalar.activation(junk[:, j % 2, :], part4(src, j), ACT.Square,
                                         accum_out=sumsq[:, n, j:j + 1]).then_inc(squared, 1)

            def h_rounded(t):
                for j in range(4):
                    act.wait_ge(transposed, 4 * t + j + 1)
                    nc.scalar.activation(
                        h_hi[:, 4 * j:4 * j + 4, t * P:(t + 1) * P],
                        bank[4 + j][:, :].rearrange("p (k c) -> p k c", c=P), ACT.Copy)\
                        .then_inc(h_hi_ready, 1)

            def x_squares(h, j):
                act.wait_ge(x_loaded[h][j], 16)
                if h == 1:
                    act.wait_ge(x_reduced, j + 1)
                nc.scalar.activation(x_sq[:, j, :, :], rows[x_half(h, j * QUARTER, QUARTER)],
                                     ACT.Square).then_inc(x_squared, 1)

            def first_split(j):
                for n in range(RAW):
                    act.wait_ge(first_loaded[n][j], 16)
                    at = (slice(None), n, slice(j * T, (j + 1) * T))
                    nc.scalar.activation(w_hi[at], raw[at], ACT.Copy).then_inc(first_hi, 1)

            def x_rounded(h, pair):
                act.wait_ge(x_normed, h * KT + 2 * pair + 2)
                at = x_half(h, 2 * pair, 2)
                nc.scalar.activation(h_hi[at], rows[at], ACT.Copy).then_inc(x_hi_ready, 1)

            for j in range(4):
                x_squares(0, j)
            for j in range(4):
                first_split(j)
            for pair in range(KT // 2):
                x_rounded(0, pair)
                if pair < 4:
                    x_squares(1, pair)
                if pair == 5:
                    split(2, 2, 1)
            split_ahead(0, 0)
            for pair in range(KT // 2):
                x_rounded(1, pair)

            act.wait_ge(vec_loaded, 16)
            with act.Fori(0, E1A) as c:
                act.wait_ge(slab_done, done(c * SLOTS + 1))
                act.wait_ge(bank_free[1], c + 1)
                nc.scalar.activation(sig, bank[0][:, :], ACT.Sigmoid).then_inc(bank_free[0], 1)
                split_ahead(c, 1)
                act.wait_ge(bank_free[1], c + 2)
                nc.scalar.activation(tile(c + CB), glu[:, PAD - CONV_B + 1:PAD - CONV_B + 1 + T],
                                     ACT.Identity, bias=col("bias_b", c),
                                     scale=tap("conv_b", c, CONV_B, 0)).then_inc(seeded_b, 1)
                split_ahead(c, 2)
                act.wait_ge(slab_done, done(c * SLOTS + 3))
                act.wait_ge(bank_free[3], c + 1)
                nc.scalar.activation(a_c, bank[2][:, :], ACT.Copy).then_inc(bank_free[2], 1)
                split_ahead(c, 3)
                act.wait_ge(bank_free[3], c + 2)
                nc.scalar.activation(tile(c), prod[:, PAD - CONV_A + 1:PAD - CONV_A + 1 + T],
                                     ACT.Identity, bias=0.0,
                                     scale=tap("conv_a", c, CONV_A, 0)).then_inc(seeded_a, 1)
                split_ahead(c + 1, 0)

            def gate(q, step, n, buf):
                act.wait_ge(slab_done, done(step * SLOTS + (q + 1)))
                act.wait_ge(gated, n + 1)
                nc.scalar.activation(sz[buf], bank[q][:, :], ACT.Silu)\
                    .then_inc(bank_free[q], 1)

            def e1b(i, first=0):
                for q in range(first, 2):
                    split_ahead(i + E1A, q)
                gate(1, i + E1A, i * 2, 0)
                split_ahead(i + E1A, 2)
                split_ahead(i + E1A, 3)
                gate(3, i + E1A, i * 2 + 1, 1)

            e1b(0, 1)
            act.wait_ge(stat_ready, 1)
            nc.scalar.activation(mean, bank[4][:, :], ACT.Copy, scale=1.0 / W_A)\
                .then_inc(bank_free[4], 1)
            with act.Fori(1, E1B) as i:
                e1b(i)

            def u_rounded(first, last):
                for k in range(first, last):
                    act.wait_ge(gated, 2 + k + 1)
                    nc.scalar.activation(h_hi[:, k, :], rows[:, k, :], ACT.Copy)\
                        .then_inc(u_hi_ready, 1)

            def e1c(i, last=False):
                for q in range(SLOTS):
                    split_ahead(i + (E1A + E1B), q)
                    c = i * 4 + q
                    act.wait_ge(ln_scaled, c + 1)
                    nc.scalar.activation(tile(c + CB), tile(c + CB), ACT.Silu,
                                         bias=col("ln_b", c), scale=col("ln_g", c))\
                        .then_inc(ln_silu, 1)
                    if last and q == SLOTS - 1:
                        act.wait_ge(h_used, 1)
                        u_rounded(0, QUARTER)
                    gate(q, i + (E1A + E1B), i * 4 + (CB + q), q % 2)

            with act.Fori(0, E1C - 1) as i:
                e1c(i)
            e1c(E1C - 1, last=True)
            u_rounded(QUARTER, KT)

            def y_squares(t, step, first, layer, sets, nb):
                if t < TT - 1:
                    act.wait_ge(acc_ready, first * (TT - 1) + (layer * NBLK * (TT - 1) + t + 1))
                else:
                    act.wait_ge(slab_done, done(step * SLOTS + SLOTS))
                nc.scalar.activation(junk_y[t], bank[t][:, :], ACT.Square,
                                     accum_out=sumsq[:, sets[t], bass.ds(nb, 1)])\
                    .then_inc(y_squared, 1)

            def blocks(at, layer, sets):
                with act.Fori(0, NBLK - 1) as nb:
                    for q in range(SLOTS):
                        split_ahead(nb + at, q)
                    for t in range(TT):
                        y_squares(t, nb + at, nb, layer, sets, nb)
                split_ahead(at + NBLK - 1, 0)

            mid_sets = [MID + 2 * t for t in range(TT)]
            blocks(AT_E2, 0, mid_sets)
            end = AT_E2 + NBLK - 1

            def mid_norm(t, between=lambda: None):
                y_squares(t, end, NBLK - 1, 0, mid_sets, NBLK - 1)
                between()
                squares(tok[:, t, :], MID + 2 * t + 1, t,
                        lambda j: act.wait_ge(x_mid_ready, 4 * t + j + 1))
                act.dma_start(x_mid[t * P:(t + 1) * P, :], tok[:, t, :]).then_inc(mid_stored, 16)

            def mid_rounded(t):
                h_rounded(t)
                if t + 2 < TT:
                    act.dma_start(resid[t % 2], x[(t + 2) * P:(t + 3) * P, :])\
                        .then_inc(resid_loaded[t % 2], 16)

            mid_norm(0)
            mid_norm(1)
            mid_rounded(0)
            mid_norm(2)
            mid_rounded(1)
            split_ahead(end, 1)

            def under_last_norm():
                mid_rounded(2)
                split_ahead(end, 2)
                split_ahead(end, 3)

            mid_norm(3, under_last_norm)
            split_ahead(end + 1, 0)
            mid_rounded(3)

            def values(g, first=0):
                for q in range(SLOTS):
                    if q >= first:
                        split_ahead(g + AT_O1, q)
                    act.wait_ge(slab_done, done(g * SLOTS + (AT_O1 * SLOTS + q + 1)))
                    act.wait_ge(v_used, g * 4 + (q + 1))
                    nc.scalar.activation(v_row[:, PAD:], bank[q][:, :], ACT.Copy)\
                        .then_inc(bank_free[q], 1)

            values(0, 1)
            with act.Fori(1, O1V) as g:
                values(g)

            def pooled_rounded(g):
                for k in range(4 * g, 4 * g + 4):
                    nc.scalar.activation(h_hi[:, k, :], rows[:, k, :], ACT.Copy)\
                        .then_inc(pool_hi_ready, 1)

            def gates(g, last=False):
                for q in range(SLOTS):
                    split_ahead(g + (AT_O1 + O1V), q)
                    if last and q == SLOTS - 1:
                        act.wait_ge(v_used, KT + 1)
                        act.wait_ge(h_used, 2)
                        pooled_rounded(0)
                    act.wait_ge(slab_done, done(g * SLOTS + ((AT_O1 + O1V) * SLOTS + q + 1)))
                    z = silu_z[:, bass.ds(g * 4 + q, 1), :].rearrange("p a t -> p (a t)")
                    nc.scalar.activation(z, bank[q][:, :], ACT.Silu).then_inc(bank_free[q], 1)

            with act.Fori(0, O1Z - 1) as g:
                gates(g)
            gates(O1Z - 1, last=True)

            def mapped_rounded(g):
                for m in range(4):
                    j = 4 * g + m
                    b = 4 + m if g % 2 else m
                    used = uses4(b, "map", g // 2) if g % 2 else AT_O1C + g // 2
                    act.wait_ge(bank_free[b], used + 2)
                    nc.scalar.activation(h_hi[:, j, :], rows[:, j, :], ACT.Copy)\
                        .then_inc(u_hi_ready, 1)

            for g in range(NG):
                if g > 0:
                    pooled_rounded(g)
                split_ahead(AT_O1C, g)
                if g > 0:
                    mapped_rounded(g - 1)
            mapped_rounded(NG - 1)

            post_sets = [POST1 + t for t in range(TT)]
            blocks(AT_O2, 1, post_sets)
            for t in range(TT):
                y_squares(t, AT_O2 + NBLK - 1, NBLK - 1, 1, post_sets, NBLK - 1)
                if t in (1, 2):
                    act.wait_ge(out_ready, 4 * t)
                    act.dma_start(resid[(t + 1) % 2], x_mid[(t + 1) * P:(t + 2) * P, :])\
                        .then_inc(resid_loaded[(t + 1) % 2], 16)

        @block.vector
        def _(dve):
            chain = [0, 0]

            def link(ins):
                chain[0] += 1
                ins.then_inc(dve_done, 1)
                dve.wait_ge(dve_done, chain[1] + chain[0])

            def split(slot, n):
                dve.wait_ge(hi_ready, n + 1)
                nc.vector.tensor_tensor(w_lo[:, slot, :], raw[:, slot % RAW, :],
                                        f32(w_hi[:, slot, :]), ALU.subtract)\
                    .then_inc(lo_ready, 1)

            def split_ahead(step, q):
                a = q + LOOKAHEAD
                split(a % SLOTS, step * SLOTS + a)

            def mean_square(n):
                link(nc.vector.reduce_sum(total[:, n:n + 1], sumsq[:, n, :], AX.X))
                nc.vector.tensor_scalar(meansq[:, n:n + 1], total[:, n:n + 1], 1.0 / D, EPS,
                                        ALU.mult, ALU.add).then_inc(mean_squared, 1)

            def scaled(dst, src, n, gain):
                dve.wait_ge(rstd_ready, n + 1)
                for j in range(4):
                    nc.vector.scalar_tensor_tensor(
                        out=part4(dst, j), in0=part4(src, j), scalar=rstd[:, n:n + 1],
                        in1=part4(gain, j), op0=ALU.mult, op1=ALU.mult).then_inc(normed, 1)

            def h_rest(t):
                for j in range(4):
                    dve.wait_ge(h_hi_ready, 4 * t + j + 1)
                    at = (slice(None), slice(4 * j, 4 * j + 4), slice(t * P, (t + 1) * P))
                    nc.vector.tensor_tensor(
                        h_lo[at], bank[4 + j][:, :].rearrange("p (k c) -> p k c", c=P),
                        f32(h_hi[at]), ALU.subtract).then_inc(bank_free[4 + j], 1)

            def make_diagonals(first, last):
                for t in range(first, last):
                    nc.vector.tensor_scalar(diagonals[:, t, :], ident[:, :],
                                            token_power[:, t:t + 1], None, ALU.mult)\
                        .then_inc(diagonals_ready, 1)

            def x_deviation(h, between=lambda: None):
                first, last = h * TT // 2, (h + 1) * TT // 2
                dve.wait_ge(x_summed, h + 1)
                for t, b in enumerate(SUM_BANKS):
                    nc.vector.tensor_scalar(token_var[:, first + t:first + t + 1],
                                            bank[b][:, 0:1], 1.0 / D, EPS, ALU.mult, ALU.add)\
                        .then_inc(bank_free[b], 1)
                between()
                dve.wait_ge(x_power_ready, h + 1)
                make_diagonals(first, last)

            def x_split(h):
                dve.wait_ge(x_spread, h + 1)
                for pair in range(KT // 2 + 1):
                    for k in range(2 * pair, min(2 * pair + 2, KT)):
                        tile_half = rows[:, k, h * HALF:(h + 1) * HALF]
                        nc.vector.scalar_tensor_tensor(
                            out=tile_half, in0=tile_half, scalar=col("pre", k),
                            in1=bank[5 + h][:, 0:HALF], op0=ALU.mult, op1=ALU.mult)\
                            .then_inc(x_normed, 1)
                    if pair > 0:
                        dve.wait_ge(x_hi_ready, h * KT // 2 + pair)
                        at = x_half(h, 2 * pair - 2, 2)
                        nc.vector.tensor_tensor(h_lo[at], rows[at], f32(h_hi[at]), ALU.subtract)\
                            .then_inc(x_lo_ready, 1)
                dve.sem_inc(bank_free[5 + h], 1)

            for j in range(4):
                dve.wait_ge(x_squared, j + 1)
                nc.vector.reduce_sum(x_partial[:, j, :],
                                     x_sq[:, j, :, :].rearrange("p k t -> p t k"), AX.X)\
                    .then_inc(x_reduced, 1)

            def first_rest(j):
                for n in range(RAW):
                    dve.wait_ge(first_hi, RAW * j + n + 1)
                    at = (slice(None), n, slice(j * T, (j + 1) * T))
                    nc.vector.tensor_tensor(w_lo[at], raw[at], f32(w_hi[at]), ALU.subtract)\
                        .then_inc(first_lo, 1)

            first_rest(0)
            x_deviation(0, lambda: first_rest(1))
            dve.wait_ge(vec_loaded, 16)
            x_split(0)
            dve.wait_ge(lo_ready, RAW + 1)
            split_ahead(0, 0)
            x_deviation(1)
            x_split(1)

            def convolve(c, taps, row, width, name, first, last):
                dst = tile(c + CB) if name == "conv_b" else tile(c)
                for j in range(first, last):
                    at = PAD - width + 1 + j
                    ins = nc.vector.scalar_tensor_tensor(
                        out=dst, in0=row[:, at:at + T], scalar=tap(name, c, width, j), in1=dst,
                        op0=ALU.mult, op1=ALU.add)
                    if taps is not None and j == width - 1:
                        ins.then_inc(taps, 1)
                    else:
                        link(ins)

            dve.wait_ge(consts_set, 6)
            before, links = chain[0], CONV_B - 2 + CONV_A - 1
            with dve.Fori(0, E1A) as c:
                chain[1] = c * links
                split_ahead(c, 1)
                dve.wait_ge(slab_done, done(c * SLOTS + 2))
                dve.wait_ge(bank_free[0], c + 2)
                nc.vector.tensor_tensor(glu[:, PAD:], bank[1][:, :], sig, ALU.mult)\
                    .then_inc(bank_free[1], 1)
                dve.wait_ge(bank_free[1], c + 2)
                dve.wait_ge(seeded_b, c + 1)
                convolve(c, conv_done, glu, CONV_B, "conv_b", 1, 11)
                split_ahead(c, 2)
                convolve(c, conv_done, glu, CONV_B, "conv_b", 11, 21)
                split_ahead(c, 3)
                dve.wait_ge(slab_done, done(c * SLOTS + 4))
                dve.wait_ge(bank_free[2], c + 2)
                nc.vector.tensor_tensor(prod[:, PAD:], bank[3][:, :], a_c, ALU.mult)\
                    .then_inc(bank_free[3], 1)
                convolve(c, conv_done, glu, CONV_B, "conv_b", 21, 25)
                split_ahead(c + 1, 0)
                convolve(c, conv_done, glu, CONV_B, "conv_b", 25, CONV_B)
                dve.wait_ge(bank_free[3], c + 2)
                dve.wait_ge(seeded_a, c + 1)
                convolve(c, None, prod, CONV_A, "conv_a", 1, CONV_A)
            assert chain[0] == before + links
            chain[:] = before + links * E1A, 0

            def e1b(i, first=0, between=None):
                step = i + E1A
                for q in range(SLOTS):
                    c = i * 2 + q // 2
                    if q >= first:
                        split_ahead(step, q)
                    if q % 2 == 0:
                        dve.wait_ge(slab_done, done(step * SLOTS + (q + 1)))
                        nc.vector.tensor_tensor(tile(c), tile(c), bank[q][:, :], ALU.mult)\
                            .then_inc(bank_free[q], 1)
                    else:
                        dve.wait_ge(bank_free[q - 1], step + 2)
                        dve.wait_ge(bank_free[q], step + 2)
                        nc.vector.tensor_tensor(tile(c), tile(c), sz[q // 2], ALU.mult)\
                            .then_inc(gated, 1)
                        if between is not None and q == 1:
                            between()

            e1b(0, first=1)
            with dve.Fori(1, E1B - 1) as i:
                e1b(i)
            dve.wait_ge(stat_ready, 2)
            nc.vector.tensor_scalar(token_var[:, :], bank[5][:, 0:TT], 1.0 / W_A, EPS,
                                    ALU.mult, ALU.add).then_inc(bank_free[5], 1)

            def layer_diagonals():
                dve.wait_ge(ln_rstd_ready, 1)
                make_diagonals(0, TT)

            e1b(E1B - 1, between=layer_diagonals)

            dve.wait_ge(stat_ready, 3)
            nc.vector.tensor_copy(ln_rstd, bank[6][:, :]).then_inc(bank_free[6], 1)
            dve.wait_ge(bank_free[6], uses4(6, "stat") + 2)

            def u_rest(j, n):
                dve.wait_ge(u_hi_ready, n + 1)
                nc.vector.tensor_tensor(h_lo[:, j, :], rows[:, j, :], f32(h_hi[:, j, :]),
                                        ALU.subtract).then_inc(u_lo_ready, 1)

            def e1c(i, last=False):
                for q in range(SLOTS):
                    c = i * 4 + q
                    nc.vector.tensor_tensor(tile(c + CB), tile(c + CB), ln_rstd, ALU.mult)\
                        .then_inc(ln_scaled, 1)
                    split_ahead(i + (E1A + E1B), q)
                    if last and q == SLOTS - 1:
                        for k in range(QUARTER):
                            u_rest(k, k)
                    dve.wait_ge(ln_silu, c + 1)
                    dve.wait_ge(bank_free[q], i + (E1A + E1B + 2))
                    nc.vector.tensor_tensor(tile(c + CB), tile(c + CB), sz[q % 2], ALU.mult)\
                        .then_inc(gated, 1)

            with dve.Fori(0, E1C - 1) as i:
                e1c(i)
            e1c(E1C - 1, last=True)
            for k in range(QUARTER, KT):
                u_rest(k, k)

            def y_gained(t, nb, count):
                dve.wait_ge(y_squared, count + (t + 1))
                nc.vector.tensor_tensor(tok[:, t, bass.ds(nb * T, T)], bank[t][:, :],
                                        gain_post[:, bass.ds(nb * T, T)], ALU.mult)\
                    .then_inc(bank_free[t], 1)

            def blocks(at, layer):
                with dve.Fori(0, NBLK - 1) as nb:
                    for q in range(SLOTS):
                        split_ahead(nb + at, q)
                    for t in range(TT):
                        y_gained(t, nb, nb * TT + layer * NBLK * TT)
                split_ahead(at + NBLK - 1, 0)

            def added(t, n, layer, used, ready, between=lambda: None):
                count = (layer * NBLK + NBLK - 1) * TT
                dve.wait_ge(y_squared, count + t + 1)
                mean_square(n)
                y_gained(t, NBLK - 1, count)
                between()
                dve.wait_ge(bank_free[t], used + 2)
                dve.wait_ge(rstd_ready, n + 1)
                dve.wait_ge(resid_loaded[t % 2], 16 * (2 * layer + t // 2 + 1))
                for j in range(4):
                    nc.vector.scalar_tensor_tensor(
                        out=part4(tok[:, t, :], j), in0=part4(tok[:, t, :], j),
                        scalar=rstd[:, n:n + 1], in1=part4(resid[t % 2], j),
                        op0=ALU.mult, op1=ALU.add).then_inc(ready, 1)

            dve.wait_ge(gain_end_loaded, 32)
            blocks(AT_E2, 0)
            end = AT_E2 + NBLK - 1

            def mid_norm(t, first=lambda: None, second=lambda: None):
                added(t, MID + 2 * t, 0, end, x_mid_ready, first)
                second()
                dve.wait_ge(squared, 4 * t + 4)
                mean_square(MID + 2 * t + 1)
                scaled(resid[t % 2], tok[:, t, :], MID + 2 * t + 1, gain_next)

            mid_norm(0)
            mid_norm(1)
            h_rest(0)
            mid_norm(2)
            h_rest(1)
            split_ahead(end, 1)

            def under_last_norm():
                h_rest(2)
                split_ahead(end, 2)

            mid_norm(3, under_last_norm, lambda: split_ahead(end, 3))
            split_ahead(end + 1, 0)
            h_rest(3)

            dve.wait_ge(mid_stored, 16 * TT)
            for g, window in enumerate(WINDOWS):
                for q in range(SLOTS):
                    j = 4 * g + q
                    if j > 0:
                        split_ahead(AT_O1 + g, q)
                    dve.wait_ge(bank_free[q], AT_O1 + g + 2)
                    src, step = v_row, 1
                    while step < window:
                        dst = sum_a if src is not sum_a else sum_b
                        link(nc.vector.tensor_tensor(
                            dst[:, PAD:], src[:, PAD:], src[:, PAD - step:PAD - step + T],
                            ALU.add))
                        src, step = dst, 2 * step
                    start = src[:, PAD:PAD + window]
                    rest = slice(PAD + window, PAD + T)
                    nc.vector.scalar_tensor_tensor(
                        out=rows[:, j, window:], in0=src[:, rest], scalar=1.0 / window,
                        in1=v_row[:, rest], op0=ALU.mult, op1=ALU.subtract)
                    link(nc.vector.tensor_tensor(start, start, inv_count[:, 0:window],
                                                       ALU.mult))
                    nc.vector.tensor_tensor(rows[:, j, 0:window], start,
                                            v_row[:, PAD:PAD + window], ALU.subtract)\
                        .then_inc(v_used, 1)
            with dve.Fori(0, O1Z) as g:
                for q in range(SLOTS):
                    split_ahead(g + (AT_O1 + O1V), q)
                    dve.wait_ge(bank_free[q], g + (AT_O1 + O1V + 2))
                    z = silu_z[:, bass.ds(g * 4 + q, 1), :].rearrange("p a t -> p (a t)")
                    nc.vector.tensor_scalar(z, z, col("c_scale", g * 4 + q), None, ALU.mult)\
                        .then_inc(z_scaled, 1)

            def group(g):
                dve.wait_ge(slab_done, done(AT_O1C * SLOTS + g + 1))
                for m in range(4):
                    j, b = 4 * g + m, (4 + m if g % 2 else m)
                    nc.vector.scalar_tensor_tensor(
                        out=rows[:, j, :], in0=bank[b][:, :], scalar=col("c_b", j),
                        in1=silu_z[:, j, :], op0=ALU.add, op1=ALU.mult)\
                        .then_inc(bank_free[b], 1)
                for j in range(4 * g, 4 * g + 4):
                    u_rest(j, KT + j)

            dve.wait_ge(z_scaled, KT)
            for g in range(NG):
                split_ahead(AT_O1C, g)
                if g > 0:
                    group(g - 1)
            group(NG - 1)

            dve.wait_ge(gain_end_loaded, 48)
            blocks(AT_O2, 1)
            for t in range(TT):
                added(t, POST1 + t, 1, AT_O2 + NBLK, out_ready)


def kernel(**inputs):
    import concourse.bacc as bacc
    from concourse.bass_utils import run_bass_kernel_spmd

    conv_b = np.asarray(inputs["e_b_conv"]).reshape(CONV_B, CB, P).transpose(2, 1, 0)
    conv_a = np.asarray(inputs["e_a_conv"]).reshape(CONV_A, CB, P).transpose(2, 1, 0)
    packed = [conv_b.reshape(P, -1), conv_a.reshape(P, -1)]
    for name, tiles in (("e_b_conv_bias", CB), ("e_b_ln_g", CB), ("e_b_ln_b", CB),
                        ("o_c_b", KT), ("o_c_scale", KT), ("e_norm_pre", KT)):
        packed.append(np.asarray(inputs[name]).reshape(tiles, P).T)
    arrays = {
        "x": np.asarray(inputs["x"]).reshape(T, D),
        "x_t": np.asarray(inputs["x"]).reshape(T, D).T,
        "vec": np.concatenate(packed, axis=1),
        "e_post": np.asarray(inputs["e_norm_post"]),
        "e_in": np.asarray(inputs["e_w_in"])[0],
        "e_out": np.asarray(inputs["e_w_out"])[0],
        "o_pre": np.asarray(inputs["o_norm_pre"]),
        "o_post": np.asarray(inputs["o_norm_post"]),
        "o_in": np.asarray(inputs["o_w_in"])[0],
        "o_cw": np.asarray(inputs["o_c_w"])[0],
        "o_out": np.asarray(inputs["o_w_out"])[0],
    }
    arrays = {name: np.ascontiguousarray(a) for name, a in arrays.items()}
    nc = bacc.Bacc("TRN2", target_bir_lowering=False, num_devices=1,
                   dynamic_dma_scratch_size=1024)
    aps = [nc.dram_tensor(name, a.shape, F32, kind="ExternalInput").ap()
           for name, a in arrays.items()]
    result = nc.dram_tensor("out", (T, D), F32, kind="ExternalOutput").ap()
    build(nc, *aps, result)
    got = run_bass_kernel_spmd(nc, [arrays], core_ids=[0]).results[0]["out"]
    return got.reshape(inputs["x"].shape)
```
